# Optimizing a Trainium2 kernel written in Bass

```python
import math
import jax, jax.numpy as jnp
from jax import lax
import numpy as np

D_MODEL = 1024
BATCH = 1
SEQ = 256
DEPTH = 1
DEC_BATCH = 8
DEC_SEQ = 1
PAST_LEN = 2048
PAGE_SIZE = 128

N_MEM = 256
CHUNK = 128
A_GROUPS = 4
A_GROUP_DIM = 128
A_WIDTH = A_GROUPS * A_GROUP_DIM
B_PAIRS = ((128, 1), (512, 4), (2048, 16))
B_HEADS_PER_GROUP = 4
B_HEADS = B_HEADS_PER_GROUP * len(B_PAIRS)
B_HEAD_DIM = 64
B_WIDTH = B_HEADS * B_HEAD_DIM
B_OUT = B_HEADS_PER_GROUP * B_HEAD_DIM
BAND_BLOCK = 128
C_HEADS = 4
C_HEAD_DIM = 128
C_WIDTH = C_HEADS * C_HEAD_DIM
N_BRANCH = 3
REL_BUCKETS = 32
REL_MAX_DIST = 2048
N_EXPERTS = 32
TOP_K = 4
D_FF = D_MODEL
SWIGLU_LIMIT = 7.0
SWIGLU_ALPHA = 1.702
MOE_BLOCK = 128
EPS = 1e-6
NEG_INF = -1e30
IN_SPLITS = (B_WIDTH, 2 * B_WIDTH, 3 * B_WIDTH, 3 * B_WIDTH + A_WIDTH, 3 * B_WIDTH + 2 * A_WIDTH, 3 * B_WIDTH + 2 * A_WIDTH + C_WIDTH)
IN_WIDTH = 3 * B_WIDTH + 2 * A_WIDTH + C_WIDTH + N_BRANCH * D_MODEL

kernel_name = 'hybrid_gmlp_dilated_moe_step'

def rmsnorm(x, g):
    xf = x.astype(jnp.float32)
    xf = xf * lax.rsqrt(jnp.mean(xf * xf, axis=-1, keepdims=True) + EPS)
    return (xf * g.astype(jnp.float32)).astype(x.dtype)

def layernorm(x, g, b):
    xf = x.astype(jnp.float32)
    xc = xf - jnp.mean(xf, axis=-1, keepdims=True)
    xf = xc * lax.rsqrt(jnp.mean(xc * xc, axis=-1, keepdims=True) + EPS)
    return (xf * g.astype(jnp.float32) + b.astype(jnp.float32)).astype(x.dtype)

def t5_bucket(dist):
    dist = np.maximum(np.asarray(dist), 0)
    max_exact = REL_BUCKETS // 2
    log_ratio = np.log(np.maximum(dist, max_exact) / max_exact) / math.log(REL_MAX_DIST / max_exact)
    large = np.minimum(max_exact + (log_ratio * (REL_BUCKETS - max_exact)).astype(np.int32), REL_BUCKETS - 1)
    return np.where(dist < max_exact, dist, large).astype(np.int32)

def chunk_spatial_gate(u, v, w_spatial, b_spatial):
    b, t, g, c = v.shape
    n_chunks = -(-t // CHUNK)
    vp = jnp.pad(v, ((0, 0), (0, n_chunks * CHUNK - t), (0, 0), (0, 0))).reshape(b, n_chunks, CHUNK, g, c)
    w_causal = jnp.where(np.tril(np.ones((CHUNK, CHUNK), bool)), w_spatial, 0.0)
    s = jnp.einsum('gij,bnjgc->bnigc', w_causal, vp) + b_spatial.T[:, :, None]
    return u * s.reshape(b, n_chunks * CHUNK, g, c)[:, :t]

def mixer_inputs(x, norm_mix, w_in, ln_v_g, ln_v_b, w_spatial, b_spatial):
    b, t, _ = x.shape
    h = rmsnorm(x, norm_mix)
    q_b, k_b, v_b, z_u, z_v, q_c, gate_logits = jnp.split(h @ w_in, IN_SPLITS, axis=-1)
    u = jax.nn.gelu(z_u).reshape(b, t, A_GROUPS, A_GROUP_DIM)
    v = layernorm(jax.nn.gelu(z_v), ln_v_g, ln_v_b).reshape(b, t, A_GROUPS, A_GROUP_DIM)
    a_out = chunk_spatial_gate(u, v, w_spatial, b_spatial).reshape(b, t, A_WIDTH)
    heads = (b, t, B_HEADS, B_HEAD_DIM)
    return (q_b.reshape(heads), k_b.reshape(heads), v_b.reshape(heads),
            q_c.reshape(b, t, C_HEADS, C_HEAD_DIM), gate_logits, a_out, v)

def dilated_band_attention(q, k, v, bias_table, window, dilation):
    b, s, h, hd = q.shape
    n = s // dilation
    reach = window // dilation
    blk = BAND_BLOCK
    nb = -(-n // blk)

    def subseq(t, front):
        t = t.reshape(b, n, dilation, h, hd).transpose(0, 2, 1, 3, 4)
        return jnp.pad(t, ((0, 0), (0, 0), (front, nb * blk - n), (0, 0), (0, 0)))

    def band(t):
        tb = subseq(t, blk).reshape(b, dilation, nb + 1, blk, h, hd)
        return jnp.concatenate([tb[:, :, :-1], tb[:, :, 1:]], axis=3)

    qb = subseq(q, 0).reshape(b, dilation, nb, blk, h, hd)
    kb, vb = band(k), band(v)
    steps = np.arange(blk)[:, None] + blk - np.arange(2 * blk)[None, :]
    key_idx = np.arange(nb)[:, None, None] * blk + np.arange(2 * blk)[None, None, :] - blk
    mask = ((steps >= 0) & (steps <= reach))[None] & (key_idx >= 0)
    bias = jnp.transpose(bias_table[t5_bucket(np.clip(steps, 0, reach) * dilation)], (2, 0, 1))
    logits = jnp.einsum('brnqhc,brnkhc->brnhqk', qb, kb).astype(jnp.float32) / math.sqrt(hd)
    logits = jnp.where(mask[:, None], logits + bias.astype(jnp.float32), NEG_INF)
    lse = jax.nn.logsumexp(logits, axis=-1)
    p = jnp.exp(logits - lse[..., None])
    out = jnp.einsum('brnhqk,brnkhc->brnqhc', p.astype(v.dtype), vb)
    out = out.reshape(b, dilation, nb * blk, h, hd)[:, :, :n].transpose(0, 2, 1, 3, 4).reshape(b, s, h, hd)
    lse = lse.transpose(0, 1, 2, 4, 3).reshape(b, dilation, nb * blk, h)[:, :, :n].transpose(0, 2, 1, 3).reshape(b, s, h)
    return out, lse

def dilated_cached_attention(q, kv_all, bias_table, window, dilation):
    b, t, h, hd = q.shape
    l = kv_all.shape[1] - t
    steps = np.arange(window // dilation + 1)
    idx = l + np.arange(t)[:, None] - steps[None, :] * dilation
    valid = idx >= 0
    kv = kv_all[:, np.maximum(idx, 0)]
    bias = bias_table[t5_bucket(steps * dilation)].T.astype(jnp.float32)
    logits = jnp.einsum('bthc,btjhc->bhtj', q, kv[:, :, :, 0]).astype(jnp.float32) / math.sqrt(hd)
    logits = jnp.where(valid[None, None], logits + bias[:, None, :], NEG_INF)
    lse = jax.nn.logsumexp(logits, axis=-1)
    p = jnp.exp(logits - lse[..., None])
    out = jnp.einsum('bhtj,btjhc->bthc', p.astype(q.dtype), kv[:, :, :, 1])
    return out, lse.transpose(0, 2, 1)

def combine_by_denominator(outs, lses):
    w = jax.nn.softmax(jnp.stack(lses), axis=0)
    o = jnp.einsum('gbth,gbthc->bthc', w.astype(outs[0].dtype), jnp.stack(outs))
    return o.reshape(o.shape[0], o.shape[1], B_OUT)

def memory_kv(mem, norm_mem, w_mem_kv):
    b, m, _ = mem.shape
    return (rmsnorm(mem, norm_mem) @ w_mem_kv).reshape(b, m, 2, C_HEADS, C_HEAD_DIM)

def memory_attention(q, mem_kv):
    b, t = q.shape[:2]
    logits = jnp.einsum('bthc,bmhc->bhtm', q, mem_kv[:, :, 0]).astype(jnp.float32) / math.sqrt(C_HEAD_DIM)
    p = jax.nn.softmax(logits, axis=-1)
    out = jnp.einsum('bhtm,bmhc->bthc', p.astype(q.dtype), mem_kv[:, :, 1])
    return out.reshape(b, t, C_WIDTH)

def merge_branches(x, a_out, b_out, c_out, gate_logits, w_branch_a, w_branch_b, w_branch_c, w_out):
    gates = jax.nn.sigmoid(gate_logits.reshape(*gate_logits.shape[:-1], N_BRANCH, D_MODEL))
    merged = (gates[..., 0, :] * (a_out @ w_branch_a) + gates[..., 1, :] * (b_out @ w_branch_b)
              + gates[..., 2, :] * (c_out @ w_branch_c))
    return x + merged @ w_out

def moe_swiglu(h, w_router, b_router, w_gate_up, b_gate_up, w_down, b_down):
    lead = h.shape[:-1]
    xt = h.reshape(-1, D_MODEL)
    n_tok = xt.shape[0]
    n_rows = n_tok * TOP_K
    logits = (xt @ w_router + b_router).astype(jnp.float32)
    top_vals, top_idx = lax.top_k(logits, TOP_K)
    gates = jax.nn.softmax(top_vals, axis=-1)
    flat_e = top_idx.reshape(-1)
    order = jnp.argsort(flat_e)
    sorted_e = flat_e[order]
    counts = jnp.bincount(flat_e, length=N_EXPERTS)
    padded = (counts + MOE_BLOCK - 1) // MOE_BLOCK * MOE_BLOCK
    start = jnp.cumsum(counts) - counts
    pend = jnp.cumsum(padded)
    dest = (pend - padded)[sorted_e] + jnp.arange(n_rows) - start[sorted_e]
    n_blocks = -(-(n_rows + N_EXPERTS * (MOE_BLOCK - 1)) // MOE_BLOCK)
    cap = n_blocks * MOE_BLOCK
    x_disp = jnp.zeros((cap, D_MODEL), xt.dtype).at[dest].set(xt[order // TOP_K])
    block_expert = jnp.clip(jnp.searchsorted(pend, jnp.arange(n_blocks) * MOE_BLOCK, side='right'), 0, N_EXPERTS - 1)

    def expert_block(args):
        xb, e = args
        gate, up = jnp.split(xb @ w_gate_up[e] + b_gate_up[e], 2, axis=-1)
        gate = jnp.minimum(gate, SWIGLU_LIMIT)
        up = jnp.clip(up, -SWIGLU_LIMIT, SWIGLU_LIMIT)
        act = gate * jax.nn.sigmoid(SWIGLU_ALPHA * gate) * (up + 1.0)
        return act @ w_down[e] + b_down[e]

    y_disp = lax.map(expert_block, (x_disp.reshape(n_blocks, MOE_BLOCK, D_MODEL), block_expert))
    y_sorted = y_disp.reshape(cap, D_MODEL)[dest]
    y_rows = jnp.zeros((n_rows, D_MODEL), y_sorted.dtype).at[order].set(y_sorted)
    y = jnp.einsum('nk,nkd->nd', gates.astype(y_rows.dtype), y_rows.reshape(n_tok, TOP_K, D_MODEL))
    return y.reshape(*lead, D_MODEL)

def channel_mixer(x, norm_ffn, w_router, b_router, w_gate_up, b_gate_up, w_down, b_down):
    return x + moe_swiglu(rmsnorm(x, norm_ffn), w_router, b_router, w_gate_up, b_gate_up, w_down, b_down)

def setup_inputs(seed: int = 0) -> dict:
    key = jax.random.key(seed)
    ks = iter(jax.random.split(key, 32))

    def nrm(shape, scale=1.0):
        return scale * jax.random.normal(next(ks), shape, jnp.float32)

    def gain(shape):
        return 1.0 + nrm(shape, 0.02)

    win_caches = [nrm((DEPTH, DEC_BATCH, min(w, PAST_LEN), 2, B_HEADS_PER_GROUP, B_HEAD_DIM)) for w, _ in B_PAIRS]
    return {
        'x_prompt': nrm((BATCH, SEQ, D_MODEL)),
        'x_sample': nrm((DEC_BATCH, DEC_SEQ, D_MODEL)),
        'cache_win0_kv': win_caches[0],
        'cache_win1_kv': win_caches[1],
        'cache_win2_kv': win_caches[2],
        'cache_mem_kv': nrm((DEPTH, DEC_BATCH, N_MEM, 2, C_HEADS, C_HEAD_DIM)),
        'mem_prompt': nrm((BATCH, N_MEM, D_MODEL)),
        'rel_bias': nrm((REL_BUCKETS, B_HEADS), 0.5),
        'norm_mix': gain((DEPTH, D_MODEL)),
        'norm_mem': gain((DEPTH, D_MODEL)),
        'w_in': nrm((DEPTH, D_MODEL, IN_WIDTH), D_MODEL ** -0.5),
        'ln_v_g': gain((DEPTH, A_WIDTH)),
        'ln_v_b': nrm((DEPTH, A_WIDTH), 0.02),
        'w_spatial': nrm((DEPTH, A_GROUPS, CHUNK, CHUNK), 0.5 * CHUNK ** -0.5),
        'b_spatial': 1.0 + nrm((DEPTH, A_GROUPS, CHUNK), 0.1),
        'w_mem_kv': nrm((DEPTH, D_MODEL, 2 * C_WIDTH), D_MODEL ** -0.5),
        'w_branch_a': nrm((DEPTH, A_WIDTH, D_MODEL), A_WIDTH ** -0.5),
        'w_branch_b': nrm((DEPTH, B_OUT, D_MODEL), B_OUT ** -0.5),
        'w_branch_c': nrm((DEPTH, C_WIDTH, D_MODEL), C_WIDTH ** -0.5),
        'w_out': nrm((DEPTH, D_MODEL, D_MODEL), D_MODEL ** -0.5),
        'norm_ffn': gain((DEPTH, D_MODEL)),
        'w_router': nrm((DEPTH, D_MODEL, N_EXPERTS), D_MODEL ** -0.5),
        'b_router': nrm((DEPTH, N_EXPERTS), 0.01),
        'w_gate_up': nrm((DEPTH, N_EXPERTS, D_MODEL, 2 * D_FF), D_MODEL ** -0.5),
        'b_gate_up': nrm((DEPTH, N_EXPERTS, 2 * D_FF), 0.02),
        'w_down': nrm((DEPTH, N_EXPERTS, D_FF, D_MODEL), D_FF ** -0.5),
        'b_down': nrm((DEPTH, N_EXPERTS, D_MODEL), 0.02),
        'norm_final': gain((D_MODEL,)),
    }

def reference(x_prompt, x_sample, cache_win0_kv, cache_win1_kv, cache_win2_kv, cache_mem_kv, mem_prompt,
              rel_bias, norm_mix, norm_mem, w_in, ln_v_g, ln_v_b, w_spatial, b_spatial, w_mem_kv,
              w_branch_a, w_branch_b, w_branch_c, w_out, norm_ffn, w_router, b_router,
              w_gate_up, b_gate_up, w_down, b_down, norm_final):
    caches = (cache_win0_kv, cache_win1_kv, cache_win2_kv)
    xp, xs = x_prompt, x_sample
    t_p = x_prompt.shape[1]
    win_p = [[] for _ in B_PAIRS]
    win_s = [[] for _ in B_PAIRS]
    mem_p, chunk_s = [], []
    for layer in range(DEPTH):
        mix_w = (norm_mix[layer], w_in[layer], ln_v_g[layer], ln_v_b[layer], w_spatial[layer], b_spatial[layer])
        merge_w = (w_branch_a[layer], w_branch_b[layer], w_branch_c[layer], w_out[layer])
        ffn_w = (norm_ffn[layer], w_router[layer], b_router[layer], w_gate_up[layer], b_gate_up[layer],
                 w_down[layer], b_down[layer])

        q_b, k_b, v_b, q_c, gate_logits, a_out, _ = mixer_inputs(xp, *mix_w)
        kv_b = jnp.stack([k_b, v_b], axis=2)
        outs, lses = [], []
        for g, (window, dilation) in enumerate(B_PAIRS):
            hs = slice(g * B_HEADS_PER_GROUP, (g + 1) * B_HEADS_PER_GROUP)
            o, l = dilated_band_attention(q_b[:, :, hs], k_b[:, :, hs], v_b[:, :, hs], rel_bias[:, hs], window, dilation)
            outs.append(o)
            lses.append(l)
            win_p[g].append(kv_b[:, t_p - min(window, t_p):, :, hs])
        mem_kv = memory_kv(mem_prompt, norm_mem[layer], w_mem_kv[layer])
        mem_p.append(mem_kv)
        xp = merge_branches(xp, a_out, combine_by_denominator(outs, lses), memory_attention(q_c, mem_kv),
                            gate_logits, *merge_w)
        xp = channel_mixer(xp, *ffn_w)

        q_b, k_b, v_b, q_c, gate_logits, a_out, v_rows = mixer_inputs(xs, *mix_w)
        kv_b = jnp.stack([k_b, v_b], axis=2)
        outs, lses = [], []
        for g, (window, dilation) in enumerate(B_PAIRS):
            hs = slice(g * B_HEADS_PER_GROUP, (g + 1) * B_HEADS_PER_GROUP)
            kv_all = jnp.concatenate([caches[g][layer], kv_b[:, :, :, hs]], axis=1)
            o, l = dilated_cached_attention(q_b[:, :, hs], kv_all, rel_bias[:, hs], window, dilation)
            outs.append(o)
            lses.append(l)
            n_all = kv_all.shape[1]
            win_s[g].append(kv_all[:, n_all - min(window, n_all):])
        chunk_s.append(v_rows)
        xs = merge_branches(xs, a_out, combine_by_denominator(outs, lses), memory_attention(q_c, cache_mem_kv[layer]),
                            gate_logits, *merge_w)
        xs = channel_mixer(xs, *ffn_w)

    y_prompt = rmsnorm(xp, norm_final)
    y_sample = rmsnorm(xs, norm_final)
    return (y_prompt, y_sample,
            jnp.stack(win_p[0]), jnp.stack(win_p[1]), jnp.stack(win_p[2]), jnp.stack(mem_p),
            jnp.stack(win_s[0]), jnp.stack(win_s[1]), jnp.stack(win_s[2]), jnp.stack(chunk_s))


_drawn_inputs = setup_inputs


def setup_inputs(seed=0):
    import zlib

    import numpy as np

    out = dict(_drawn_inputs(seed))
    spreads = {}
    factors = {'norm_mem': 2.837,
     'ln_v_b': 7.742,
     'b_gate_up': 5.429,
     'b_down': 6.248,
     'norm_final': 29.684,
     'ln_v_g': 7.247}
    for name, (base, spread) in spreads.items():
        noise = np.random.default_rng([zlib.crc32(name.encode()), seed]).standard_normal(out[name].shape)
        drawn = base * np.exp(spread * noise) if base else spread * noise
        out[name] = __import__('jax').numpy.asarray(drawn.astype(out[name].dtype))
    for name, factor in factors.items():
        out[name] = (out[name] * factor).astype(out[name].dtype)
    return out
```

```python
import math
from contextlib import ExitStack

import concourse.bass as bass
import numpy as np
from concourse import mybir

F32 = mybir.dt.float32
I32 = mybir.dt.int32
U32 = mybir.dt.uint32
ALU = mybir.AluOpType
ACT = mybir.ActivationFunctionType
AX = mybir.AxisListType

P = 128
D = 1024
KD = D // P
SEQ = 256
NS = 8
NT = SEQ + NS
TILES = ((0, 128), (128, 128), (256, NS))
PAIRS = ((128, 1), (512, 4), (2048, 16))
NG = len(PAIRS)
HPG = 4
NH = NG * HPG
HD = 64
BW = NH * HD
REL_BUCKETS = 32
REL_MAX_DIST = 2048
AG = 4
NM = 256
CH = 4
CD = 128
E = 32
TOPK = 4
EPS = 1e-6
NEG = -1e30
LIMIT = 7.0
ALPHA = 1.702
C_SCALE = 1.0 / math.sqrt(CD)
B_SCALE = 1.0 / math.sqrt(HD)
SLOTS = 64
PASSES = -(-NT // SLOTS)
GU = 2 * D // P
CHUNKS = KD + KD // 2
HANK = 384
QO, KO, VO, UO, ZO, CO, GO = 0, BW, 2 * BW, 3 * BW, 3 * BW + 512, 3 * BW + 1024, 3 * BW + 1536


def t5_bucket(dist):
    dist = np.maximum(np.asarray(dist), 0)
    exact = REL_BUCKETS // 2
    ratio = np.log(np.maximum(dist, exact) / exact) / math.log(REL_MAX_DIST / exact)
    large = np.minimum(exact + (ratio * (REL_BUCKETS - exact)).astype(np.int32), REL_BUCKETS - 1)
    return np.where(dist < exact, dist, large).astype(np.int32)


def shape_constants():
    c = np.zeros((P, 4 * P + 3), np.float32)
    c[:, 0:P] = np.eye(P)
    c[:, P:2 * P] = np.triu(np.ones((P, P)))
    c[:, 2 * P:3 * P] = np.triu(np.ones((P, P)), 1)
    c[:, 3 * P:4 * P] = np.eye(P)[::-1]
    c[:, 4 * P] = c[:, 4 * P + 1] = 1
    c[:NS, 4 * P + 2] = 1
    hank = np.zeros((REL_BUCKETS + 1, NG, HANK), np.float32)
    dist = 2 * P - 1 - np.arange(HANK)
    for g, (window, dilation) in enumerate(PAIRS):
        ok = (dist >= 0) & (dist % dilation == 0) & (dist <= window)
        hank[t5_bucket(dist), g, np.arange(HANK)] = ok
        hank[REL_BUCKETS, g] = np.where(ok, 0, NEG)
    samp = np.zeros((REL_BUCKETS, NG + 1, P), np.float32)
    for g, (window, dilation) in enumerate(PAIRS):
        samp[t5_bucket((P - np.arange(P)) * dilation), g, np.arange(P)] = 1
    samp[t5_bucket(0), NG] = 1
    return {"square": c, "hankel": hank.reshape(REL_BUCKETS + 1, -1), "sample": samp.reshape(REL_BUCKETS, -1)}


def mixer_blocks(w_in, w_mem_kv, w_branch_a, w_branch_b, w_branch_c, w_out):
    def cols(w, a, b):
        return w[0, :, a:b].rearrange("(k p) c -> p k c", p=P)

    def whole(w, p):
        return w[0].rearrange("(k p) c -> p k c", p=p)

    out = [("memk", cols(w_mem_kv, 0, 512)), ("memv", cols(w_mem_kv, 512, 1024))]
    out += [("in0", cols(w_in, 0, 512)), ("in1", cols(w_in, 512, 1024)), ("in2", cols(w_in, 1024, 1536))]
    out += [("v0", cols(w_in, VO, VO + 512)), ("v1", cols(w_in, VO + 512, VO + 768))]
    out += [("qc", cols(w_in, CO, CO + 512)), ("zv", cols(w_in, ZO, ZO + 512)), ("zu", cols(w_in, UO, UO + 512))]
    for n, (i, w, p) in {"a": (0, w_branch_a, P), "c": (2, w_branch_c, P), "b": (1, w_branch_b, HD)}.items():
        g = GO + i * D
        out += [("g" + n + "0", cols(w_in, g, g + 512)), ("w" + n, whole(w, p)), ("g" + n + "1", cols(w_in, g + 512, g + D))]
    out += [("o0", cols(w_out, 0, 512)), ("o1", cols(w_out, 512, 1024))]
    return out


def schedule():
    s = [("vec",), ("wsp",)] + [("rel", g) for g in range(NG)] + [("sbias",)]
    s += [("memT", k) for k in range(KD)] + [("kc", h) for h in range(CH)] + [("xT", k) for k in range(KD)]
    s += [("vc", t) for t in range(2)] + [("kct", t) for t in range(2)]
    s += [("q", m) for m in range(6)] + [("k", m) for m in range(6)]
    s += [("v", t, 0) for t in range(3)] + [("v", t, 1) for t in range(3)]
    s += [("kt", t, n) for t in range(3) for n in range(2)] + [("qc", m) for m in range(4)]
    s += [("qs", 0), ("qs", 1), ("qcs",), ("vts",), ("selfb",)]
    big = [("zv", t) for t in range(3)] + [("zu", m) for m in range(4)]
    for b in range(NS):
        s += [("sk", b, 0), ("sk", b, 1), ("skc", b)]
        if b < len(big):
            s += [big[b]]
    s += [("norm_v",), ("vat",), ("sp", 0), ("sp", 1), ("sp", 2), ("sp", 3), ("slog",)]
    units = [("C", h, t) for t in range(2) for h in range(CH)] + [("B", h, t) for t in range(2) for h in range(HPG)]
    for n in range(len(units) + 2):
        if n < len(units):
            s += [("score", n, units[n])]
        if n < 16:
            s += [("p" if n % 2 == 0 else "g", "a", n // 2)]
        if 1 <= n <= len(units):
            s += [("turn", n - 1, units[n - 1])]
        if n >= 2:
            s += [("mix", n - 2, units[n - 2])]
        if n == 4:
            s += [("ssum",)]
    for b in range(NS):
        s += [("sv", b)]
    for br in "cb":
        for m in range(KD):
            s += [("p", br, m), ("g", br, m)]
    s += [("wo", t, n) for n in range(2) for t in range(3)]
    s += [("norm_f",)] + [("brow", n) for n in range(3)] + [("hT", k) for k in range(KD)]
    s += [("rt", t) for t in range(3)] + [("top",), ("pos",)]
    return s


ROTATING = {"vec", "wsp", "rel", "sbias", "memT", "kc", "xT", "vc", "kct", "q", "k", "v", "kt", "qc", "qs", "qcs", "vts",
            "selfb", "sk", "skc", "zv", "zu", "vat", "sp", "p", "g", "ssum", "sv", "wo", "brow", "hT", "rt", "pos"}
LAST_USE = {("kc", 3): 0, ("vc", 1): 1, ("q", 3): 2, ("k", 1): 3, ("k", 5): 4, ("v", 2, 0): 5, ("v", 2, 1): 6, ("qc", 3): 7,
            ("zv", 2): 8, ("zu", 3): 9}
for _n, _br in enumerate("acb"):
    LAST_USE[("g", _br, 3)] = 10 + 3 * _n
    LAST_USE[("p", _br, 7)] = 11 + 3 * _n
    LAST_USE[("g", _br, 7)] = 12 + 3 * _n
LAST_USE[("wo", 2, 0)] = 19
LAST_USE[("wo", 2, 1)] = 20


def build(nc, I, C, O):
    blocks = mixer_blocks(*(I[n] for n in ("w_in", "w_mem_kv", "w_branch_a", "w_branch_b", "w_branch_c", "w_out")))
    block_at = {name: n for n, (name, _) in enumerate(blocks)}
    steps = schedule()
    job = {s: n for n, s in enumerate([s for s in steps if s[0] in ROTATING])}
    last_job = {n: job[s] + 1 for s, n in LAST_USE.items()}
    caches = [I[f"cache_win{g}_kv"] for g in range(NG)]

    with ExitStack() as ctx:
        def sb(name, shape, dt=F32):
            return ctx.enter_context(nc.sbuf_tensor(name, shape, dt))

        def sem(name):
            return ctx.enter_context(nc.semaphore(name))

        ring = sb("ring", [P, 12 * 2048])

        def block_view(name, p=P):
            n = block_at[name] % 4
            k = blocks[block_at[name]][1].shape[1]
            c = blocks[block_at[name]][1].shape[2]
            return ring[0:p, n * 4096:n * 4096 + k * c].rearrange("p (k c) -> p k c", k=k)

        def chunk_slot(k):
            return (k + 8) % CHUNKS

        def chunk_view(k):
            s = chunk_slot(k)
            return ring[:, s * 2048:(s + 1) * 2048]

        scratch = ring[:, 8 * 2048:12 * 2048]
        kv_b = [scratch[:, n * 1792:n * 1792 + 768].rearrange("p (g c) -> p g c", g=NG) for n in range(2)]
        kv_c = [scratch[:, n * 1792 + 768:(n + 1) * 1792].rearrange("p (t c) -> p t c", t=2) for n in range(2)]
        probs = [scratch[:, 3584 + n * 768:3584 + (n + 1) * 768] for n in range(2)]
        probs_t = [scratch[:, 5120 + n * 768:5120 + (n + 1) * 768] for n in range(2)]
        mem_tok = scratch[:, 3584:3584 + 2048].rearrange("p (t c) -> p t c", t=2)
        prod = scratch[:, 6656:6656 + 1024]

        hT = sb("hT", [P, KD, NT])
        acc = hT
        merged = sb("merged", [P, KD, NT])
        memT = merged[:, :, 0:NM]
        x1 = sb("x1", [P, 3, D])
        hank = x1[:, :, :].rearrange("p t c -> p (t c)").rearrange("p (h k) -> p h k", h=NH)
        qk = sb("qk", [P, 12, NT])
        qT, kT = qk[:, 0:6, :], qk[:, 6:12, :]
        qcT = sb("qcT", [P, CH, NT])
        kvt = sb("kvt", [P, 2 * 3 * BW])
        k_tok = kvt[:, 0:3 * BW].rearrange("p (t c) -> p t c", t=3)
        v_tok = kvt[:, 3 * BW:6 * BW].rearrange("p (t c) -> p t c", t=3)
        kc = sb("kc", [P, CH * NM + 2 * 1024])
        kcT = kc[:, 0:CH * NM].rearrange("p (h m) -> p h m", h=CH)
        kvc = kc[:, CH * NM:].rearrange("p (t c) -> p t c", t=2)
        uT = sb("uT", [P, AG, NT])
        va = sb("va", [P, 3, 512])
        bT_all = sb("bT", [P, HPG * NT])
        bT = bT_all[0:HD, :].rearrange("p (h t) -> p h t", h=HPG)
        lnw = bT_all[:, 0:1024].rearrange("p (a c) -> p a c", a=2)
        sq = sb("sq", [P, 4 * P + 3])
        ident, triu, before, flip, valid = (sq[:, 0:P], sq[:, P:2 * P], sq[:, 2 * P:3 * P], sq[:, 3 * P:4 * P],
                                            sq[:, 4 * P:4 * P + 3])
        ones = sb("ones", [P, P])
        wspT = sb("wspT", [P, AG, P])
        wsp = sb("wsp", [P, AG, P])
        bsp = sb("bsp", [P, AG, P])
        w00 = sb("w00", [P, AG])
        vecr = sb("vecr", [3 * KD, P])
        vec = sb("vec", [P, 3 * KD])
        g_mix, g_mem, g_ffn = vec[:, 0:KD], vec[:, KD:2 * KD], vec[:, 2 * KD:3 * KD]
        rel = sb("rel", [REL_BUCKETS + 1, NH])
        selh = va[0:REL_BUCKETS + 1, :, :].rearrange("p t c -> p (t c)")[:, 0:NG * HANK].rearrange("p (g x) -> p g x", g=NG)
        pair = sb("pair", [P, 2 * NT])
        sels = pair[0:REL_BUCKETS, 0:(NG + 1) * P].rearrange("p (g x) -> p g x", g=NG + 1)
        hrow = scratch[0:HPG, 6656:6656 + NG * HANK].rearrange("p (g x) -> p g x", g=NG)
        stat = sb("stat", [P, 40])
        bn = sb("bn", [P, 3, 6])
        bna = sb("bna", [P, 3, 2])
        flat = merged[:, :, :].rearrange("p k t -> p (k t)")
        qs, slf = flat[0:NS, 0:BW + 512], flat[0:NS, BW + 512:2 * BW + 512]
        sbias = sb("sbias", [P, 2 * NH])
        slog = sb("slog", [NS, NH])
        sdiag = sb("sdiag", [NS, NS, NH])
        samp = sb("samp", [P, NS * NH + NS * 2 * CH])
        sB, sC = samp[:, 0:NS * NH], samp[:, NS * NH:]
        smax = sb("smax", [P, NS * NH + NS * 2 * CH])
        stop = sb("stop", [P, NS * HPG + NS * CH])
        stot = sb("stot", [P, NS * HPG + NS * CH])
        sself = sb("sself", [P, NS * NH])
        vts = sb("vts", [HD, NH, NS])
        vself = sb("vself", [HD, HPG, NS])
        th = [sb(f"th{n}", [P, NT]) for n in range(2)]
        tmp = [pair[:, n * NT:(n + 1) * NT] for n in range(2)]
        wr = sb("wr", [P, KD, E])
        br = sb("br", [P, E])

        xr = kvt[:, 0:3 * D].rearrange("p (t c) -> p t c", t=3)
        gfin = kvt[:, 3 * D:4 * D]
        sel_p = kvt[:, 4 * D:4 * D + 192].rearrange("p (t s) -> p t s", t=3)
        sel_g = kvt[:, 4 * D + 192:4 * D + 384].rearrange("p (t s) -> p t s", t=3)
        moe = qk[:, :, :].rearrange("p a b -> p (a b)")
        xg, gate, up, sig, actv, yT = (moe[:, n * 512:(n + 1) * 512].rearrange("p (k s) -> p k s", k=KD) for n in range(6))
        y_tok = uT[0:SLOTS, :, :].rearrange("p a b -> p (a b)")[:, 0:D]
        gT = bT_all[0:SLOTS, 0:NT]
        brow = kc[0:E, 0:3 * D]
        bexp = qcT[:, :, :].rearrange("p a b -> p (a b)")[:, 0:3 * KD * E].rearrange("p (k e) -> p k e", e=E)
        small = va[:, :, :].rearrange("p a b -> p (a b)")
        lg = small[:, 0:96].rearrange("p (t e) -> p t e", t=3)
        mx8 = small[:, 96:120].rearrange("p (t e) -> p t e", t=3)
        idf = small[:, 120:144].rearrange("p (t e) -> p t e", t=3)
        gk = small[:, 144:156].rearrange("p (t j) -> p t j", t=3)
        gsum = small[:, 156:159]
        eq = small[:, 192:192 + 384].rearrange("p (t e j) -> p t e j", t=3, e=E)
        msk = small[:, 576:672].rearrange("p (t e) -> p t e", t=3)
        gw = small[:, 672:768].rearrange("p (t e) -> p t e", t=3)
        posm = small[:, 768:768 + 99].rearrange("p (t e) -> p t e", t=3)
        iota = sb("iota", [P, SLOTS * PASSES])
        most = small[0:1, 1208:1209]
        idx = sb("idx", [P, 3, 8], U32)
        over = sb("over", [1, 1], I32)

        bank = [ctx.enter_context(nc.psum_tensor(f"bank{n}", [P, 512], F32)) for n in range(4)]
        wide = [ctx.enter_context(nc.psum_tensor(f"wide{n}", [P, 1024], F32)) for n in range(2)]
        rel_rows = nc.dram_tensor("rel_rows", [NG, HPG, HANK], F32)

        s_sq, s_vecr, s_wsp, s_rel, s_sels, s_lnw, s_bsp, s_w00 = (sem("in_" + n) for n in (
            "square", "vectors", "wsp", "rel", "sample", "lnw", "bsp", "w00"))
        s_router_in, s_gfin_in, s_brow_in = sem("in_router"), sem("in_gfin"), sem("in_brow")
        s_mem_in, s_x_in, s_xagain = sem("in_mem"), sem("in_x"), sem("in_x_again")
        s_block_in = [sem(f"block_in{n}") for n in range(4)]
        s_chunk_in = [sem(f"chunk_in{n}") for n in range(CHUNKS)]
        s_chunk_used = sem("chunk_used")
        s_job = sem("job_done")
        s_taken = [sem(f"taken{n}") for n in range(3)]
        s_done = {n: sem("ready_" + n) for n in (
            "ones", "vec", "wspT", "rel_aug", "hrow", "sbias", "xn", "memn", "memT", "xT", "kcT", "kvc", "q", "k", "v", "ktok", "qc",
            "qs", "vts", "sdiag", "selfb", "sk", "va", "vraw", "uT", "aT", "sexp", "sprob", "parmax", "bs", "cs", "th", "merged",
            "x1", "xr", "hTf", "logits", "masks", "posm", "bexp", "lgs")}
        s_hstore, s_hank, s_kv_in, s_kv_used, s_out = sem("hankel_stored"), sem("in_hankel"), sem("kv_in"), sem("kv_used"), sem("out")
        s_kvin = [sem(f"kv_in{n}") for n in range(2)]
        s_kvout, s_kvcout, s_vaout = sem("out_kv"), sem("out_memkv"), sem("out_chunk_v")
        s_copy = sem("out_shift")
        s_score, s_max, s_exp, s_prob, s_turned, s_pt, s_mixed, s_mixout = (sem("att_" + n) for n in (
            "scores", "max", "exp", "probs", "turned", "probs_t", "mixed", "out"))
        s_ss, s_ms, s_rt, s_rs = sem("sum_squares"), sem("mean_square"), sem("root"), sem("inv_root")
        s_tmax, s_texp = sem("top_shifted"), sem("top_exp")
        s_accout = sem("experts_summed")
        s_dve, s_act = sem("dve_step"), sem("act_step")
        s_p, s_pg, s_gath, s_xg, s_gate, s_sig, s_actv, s_yT, s_yturn, s_ytok, s_gturn, s_gT, s_scat, s_acc, s_loop = (
            sem("moe_" + n) for n in ("select", "gated_select", "gathered", "x", "gate", "sigmoid", "act", "yT", "y_turned",
                                      "y_tok", "g_turned", "gT", "scattered", "added", "dve_step"))
        s_iota = sem("iota")
        s_carry = sem("waits_carried")
        s_finj, s_fin, s_finT = sem("final_turned"), sem("final_rows"), sem("final_added")

        def taken(eng, *s):
            eng.wait_ge(s_taken[job[s] % 3], job[s] // 3 + 1)

        block = ctx.enter_context(nc.Block())

        @block.sync
        def _(sp):
            with nc.allow_non_contiguous_dma(reason="small vectors"):
                sp.dma_start(mem_tok, I["mem_prompt"][0].rearrange("(t p) c -> p t c", p=P)).then_inc(s_mem_in, 16)
                sp.dma_start(x1[:, 0:2, :], I["x_prompt"][0].rearrange("(t p) c -> p t c", p=P)).then_inc(s_x_in, 16)
                sp.dma_start(x1[0:NS, 2, :], I["x_sample"][:, 0, :]).then_inc(s_x_in, 16)
            copies = []
            for b in range(NS):
                copies.append((2, slice(b, b + 1)))
                if b == 3:
                    copies.append((1, slice(0, 4)))
            copies += [(1, slice(4, 8)), (0, slice(0, 8))]

            def shift(g, bs):
                w = PAIRS[g][0]
                src = caches[g][0, bs, 1:w].rearrange("b w a h c -> b (w a h c)")
                dst = O[6 + g][0, bs, 0:w - 1].rearrange("b w a h c -> b (w a h c)")
                sp.dma_start(dst, src).then_inc(s_copy, 16)

            for n, (name, src) in enumerate(blocks):
                if n >= 4:
                    sp.wait_ge(s_job, last_job[n - 4])
                sp.dma_start(block_view(name, src.shape[0]), src).then_inc(s_block_in[n % 4], 16)
                if 2 <= n and copies:
                    shift(*copies.pop(0))
                if name == "gc1":
                    sp.wait_ge(s_mixed, 2 * (CH + HPG))
                    sp.dma_start(x1[:, 0:2, :], I["x_prompt"][0].rearrange("(t p) c -> p t c", p=P)).then_inc(s_xagain, 16)
                    sp.dma_start(x1[0:NS, 2, :], I["x_sample"][:, 0, :]).then_inc(s_xagain, 16)
                    sp.wait_ge(s_kvcout, 16)
                    sp.dma_start(brow[:, 0:2 * D], I["b_gate_up"][0]).then_inc(s_brow_in, 16)
                    sp.dma_start(brow[:, 2 * D:3 * D], I["b_down"][0]).then_inc(s_brow_in, 16)
            for c in copies:
                shift(*c)

            def chunk(e, k):
                s = chunk_slot(k)
                if k < KD:
                    src = I["w_gate_up"][0, e, k * P:(k + 1) * P, :]
                    dst = chunk_view(k)
                else:
                    r = (k - KD) * 2 * P
                    src = I["w_down"][0, e, r:r + 2 * P, :].rearrange("(j p) c -> p j c", p=P)
                    dst = chunk_view(k).rearrange("p (j c) -> p j c", j=2)
                sp.dma_start(dst, src).then_inc(s_chunk_in[s], 16)

            def chunk_dyn(e, k):
                s = chunk_slot(k)
                if k < KD:
                    src = I["w_gate_up"][0, bass.ds(e, 1), k * P:(k + 1) * P, :].rearrange("e p c -> p (e c)")
                    dst = chunk_view(k)
                else:
                    r = (k - KD) * 2 * P
                    src = I["w_down"][0, bass.ds(e, 1), r:r + 2 * P, :].rearrange("e (j p) c -> p (e j) c", p=P)
                    dst = chunk_view(k).rearrange("p (j c) -> p j c", j=2)
                sp.dma_start(dst, src).then_inc(s_chunk_in[s], 16)

            sp.wait_ge(s_mixed, 2 * (CH + HPG))
            sp.wait_ge(s_mixout, 2 * (CH + HPG))
            sp.wait_ge(s_kv_used, 2 * NS)
            for k in range(4):
                chunk(0, k)
            for k, n in ((4, 20), (5, 20), (6, 17), (7, 17), (8, 18), (9, 18), (10, 19), (11, 19)):
                sp.wait_ge(s_job, last_job[n])
                chunk(0, k)
            with sp.Fori(1, E) as e:
                for k in range(CHUNKS):
                    sp.wait_ge(s_chunk_used, e * CHUNKS + (k - CHUNKS + 1))
                    chunk_dyn(e, k)
            sp.wait_ge(s_done["posm"], 1)
            flag = sp.value_load(over[0:1, 0:1], min_val=0, max_val=NT)
            with sp.If(flag > SLOTS):
                with sp.Fori(1, PASSES) as ps:
                    with sp.Fori(0, E) as e:
                        for k in range(CHUNKS):
                            sp.wait_ge(s_chunk_used, ps * (E * CHUNKS) + e * CHUNKS + (k - CHUNKS + 1))
                            chunk_dyn(e, k)
            sp.wait_ge(s_fin, 1)
            sp.dma_start(O[0][0, 0:P], x1[:, 0, :]).then_inc(s_out, 16)
            sp.wait_ge(s_fin, 2)
            sp.dma_start(O[0][0, P:2 * P], x1[:, 1, :]).then_inc(s_out, 16)
            sp.wait_ge(s_fin, 3)
            sp.dma_start(O[1][:, 0, :], x1[0:NS, 2, :]).then_inc(s_out, 16)
            sp.wait_ge(s_out, 48)
            sp.wait_ge(s_copy, 16 * 11)

        @block.gpsimd
        def _(pool):
            nc.gpsimd.iota(iota[:], [[1, SLOTS * PASSES]], base=0, channel_multiplier=0,
                           allow_small_or_imprecise_dtypes=True).then_inc(s_iota, 1)
            taken(pool, "rel", NG - 1)
            pool.dma_start(rel_rows[:].rearrange("g h x -> h g x"), hrow).then_inc(s_hstore, 16)
            pool.wait_ge(s_hstore, 16)
            src = bass.AP(rel_rows, 0, [[1, P], [HANK, NH], [1, 2 * P]])
            taken(pool, "xT", KD - 1)
            pool.dma_start(hank, src).then_inc(s_hank, 16)

            def stream(n):
                b, a = n % NS, n // NS
                if n >= 2:
                    pool.wait_ge(s_kv_used, n - 1)
                for g, (w, dil) in enumerate(PAIRS):
                    src = caches[g][0, b, :, a].rearrange("(j r) h c -> j r (h c)", r=dil)[:, 0, :]
                    pool.dma_start(kv_b[n % 2][:, g, :], src).then_inc(s_kvin[n % 2], 16)
                src = I["cache_mem_kv"][0, b, :, a].rearrange("(t p) h c -> p t (h c)", p=P)
                pool.dma_start(kv_c[n % 2], src).then_inc(s_kvin[n % 2], 16)

            stream(0)
            stream(1)
            taken(pool, "kct", 1)
            dst = O[5][0, 0].rearrange("(t p) a h c -> p t (a h c)", p=P)
            pool.dma_start(dst, kvc).then_inc(s_kvcout, 16)
            taken(pool, "v", 2, 1)
            taken(pool, "kt", 2, 1)
            for a, rows in ((0, k_tok), (1, v_tok)):
                for g, (w, _) in enumerate(PAIRS):
                    c = slice(g * 256, (g + 1) * 256)
                    first = 0 if w >= SEQ else 1
                    dst = O[2 + g][0, 0, :, a].rearrange("(t p) h c -> p t (h c)", p=P)
                    pool.dma_start(dst, rows[:, first:2, c]).then_inc(s_kvout, 16)
                    pool.dma_start(O[6 + g][0, :, w - 1, a].rearrange("b h c -> b (h c)"), rows[0:NS, 2, c]).then_inc(s_kvout, 16)
            for n in range(2, NS + 2):
                stream(n)
            pool.wait_ge(s_done["va"], 1)
            pool.dma_start(O[9][0, :, 0].rearrange("b g c -> b (g c)"), va[0:NS, 2, :]).then_inc(s_vaout, 16)
            pool.wait_ge(s_done["lgs"], 1)
            nc.gpsimd.partition_all_reduce(smax[:], samp[:], P, bass.bass_isa.ReduceOp.max).then_inc(s_done["parmax"], 1)
            for n in range(NS + 2, 2 * NS):
                stream(n)
            pool.wait_ge(s_kvcout, 16)
            pool.wait_ge(s_kvout, 16 * 12)
            pool.wait_ge(s_vaout, 16)

        @block.tensor
        def _(pe):
            def mm(out, lhsT, rhs, start=True, stop=True, **kw):
                return nc.tensor.matmul(out, lhsT, rhs, start=start, stop=stop, **kw)

            def turn(out, in_, n):
                return nc.tensor.transpose(out, in_, ident[0:n, 0:n])

            landed = set()

            def weights(name):
                n = block_at[name]
                if name not in landed:
                    pe.wait_ge(s_block_in[n % 4], 16 * (n // 4 + 1))
                    landed.add(name)
                return block_view(name, blocks[n][1].shape[0])

            def wide_tile(out, w, m, rhs, kn=KD):
                for k in range(kn):
                    last = mm(out, w[:, k, m * P:(m + 1) * P], rhs[:, k, :], k == 0, k == kn - 1)
                return last

            def row_tile(out, lhs, w, t, n):
                t0, tn = TILES[t]
                for k in range(KD):
                    last = mm(out[0:tn, 0:n], lhs[:, k, t0:t0 + tn], w[:, k, 0:n], k == 0, k == KD - 1)
                return last

            pe.wait_ge(s_sq, 16)
            pe.wait_ge(s_done["ones"], 2)
            for s in steps:
                kind, a = s[0], s[1:]
                if kind in ROTATING:
                    n = job[s]
                    o = bank[n % 3]
                    if n >= 3:
                        pe.wait_ge(s_taken[n % 3], n // 3)
                if kind == "vec":
                    pe.wait_ge(s_vecr, 48)
                    last = turn(o[:, 0:3 * KD], vecr[:], 3 * KD)
                elif kind == "wsp":
                    pe.wait_ge(s_wsp, 16)
                    for g in range(AG):
                        last = turn(o[:, g * P:(g + 1) * P], wsp[:, g, :], P)
                elif kind == "rel":
                    g, = a
                    pe.wait_ge(s_rel, 32)
                    last = mm(o[0:HPG, 0:HANK], rel[:, g * HPG:(g + 1) * HPG], selh[:, g, :])
                elif kind == "sbias":
                    pe.wait_ge(s_sels, 16)
                    for g in range(NG):
                        h4 = slice(g * HPG, (g + 1) * HPG)
                        mm(o[:, h4], sels[:, g, :], rel[0:REL_BUCKETS, h4])
                    last = mm(o[:, NH:2 * NH], sels[:, NG, :], rel[0:REL_BUCKETS, :])
                elif kind == "memT":
                    k, = a
                    pe.wait_ge(s_done["memn"], 1)
                    for t in range(2):
                        last = turn(o[:, t * P:(t + 1) * P], mem_tok[:, t, k * P:(k + 1) * P], P)
                elif kind == "xT":
                    k, = a
                    pe.wait_ge(s_done["xn"], 1)
                    for t, (t0, tn) in enumerate(TILES):
                        last = turn(o[:, t0:t0 + tn], x1[0:tn, t, k * P:(k + 1) * P], tn)
                elif kind == "kc":
                    taken(pe, "memT", KD - 1)
                    last = wide_tile(o[:, 0:NM], weights("memk"), a[0], memT)
                elif kind == "vc":
                    t, = a
                    w = weights("memv")
                    for k in range(KD):
                        last = mm(o[:], memT[:, k, t * P:(t + 1) * P], w[:, k, :], k == 0, k == KD - 1)
                elif kind == "kct":
                    t, = a
                    taken(pe, "kc", CH - 1)
                    for h in range(CH):
                        last = turn(o[:, h * P:(h + 1) * P], kcT[:, h, t * P:(t + 1) * P], P)
                elif kind in ("q", "k"):
                    taken(pe, "xT", KD - 1)
                    c = a[0] + (0 if kind == "q" else 6)
                    last = wide_tile(o[:, 0:NT], weights(f"in{c // 4}"), c % 4, hT)
                elif kind == "v":
                    t, n = a
                    last = row_tile(o, hT, weights(f"v{n}"), t, (512, 256)[n])
                elif kind == "kt":
                    t, n = a
                    t0, tn = TILES[t]
                    taken(pe, "k", 5)
                    for i in range(3):
                        last = turn(o[0:tn, i * P:(i + 1) * P], kT[:, 3 * n + i, t0:t0 + tn], P)
                elif kind == "qc":
                    last = wide_tile(o[:, 0:NT], weights("qc"), a[0], hT)
                elif kind == "qs":
                    n, = a
                    taken(pe, "q", 5)
                    for i in range(3):
                        last = turn(o[0:NS, i * P:(i + 1) * P], qT[:, 3 * n + i, SEQ:NT], P)
                elif kind == "qcs":
                    taken(pe, "qc", CH - 1)
                    for h in range(CH):
                        last = turn(o[0:NS, h * P:(h + 1) * P], qcT[:, h, SEQ:NT], P)
                elif kind == "vts":
                    taken(pe, "v", 2, 1)
                    for h in range(NH):
                        last = turn(o[0:HD, h * NS:(h + 1) * NS], v_tok[0:NS, 2, h * HD:(h + 1) * HD], NS)
                elif kind == "selfb":
                    pe.wait_ge(s_done["sdiag"], 1)
                    last = mm(o[:, 0:NS * NH], ones[0:NS, :], sdiag[:].rearrange("p b h -> p (b h)"))
                elif kind == "sk":
                    b, n = a
                    taken(pe, "qcs")
                    last = mm(o[:, 0:384], ident[0:NS, b:b + 1].to_broadcast([NS, P]), qs[:, n * 384:(n + 1) * 384])
                elif kind == "skc":
                    last = mm(o[:], ident[0:NS, a[0]:a[0] + 1].to_broadcast([NS, P]), qs[:, BW:BW + 512])
                elif kind == "zv":
                    last = row_tile(o, hT, weights("zv"), a[0], 512)
                elif kind == "zu":
                    last = wide_tile(o[:, 0:NT], weights("zu"), a[0], hT)
                elif kind == "vat":
                    pe.wait_ge(s_done["va"], 1)
                    for g in range(AG):
                        last = turn(o[:, g * NS:(g + 1) * NS], va[0:NS, 2, g * P:(g + 1) * P], NS)
                elif kind == "sp":
                    g, = a
                    for t in range(2):
                        last = mm(o[:, t * P:(t + 1) * P], va[:, t, g * P:(g + 1) * P], wspT[:, g, :])
                elif kind == "p":
                    br_, m = a
                    if br_ == "a":
                        pe.wait_ge(s_done["aT"], 1 + AG)
                        last = wide_tile(o[:, 0:NT], weights("wa"), m, uT, AG)
                    elif br_ == "c":
                        taken(pe, "sv", NS - 1)
                        pe.wait_ge(s_mixout, 2 * (CH + HPG))
                        last = wide_tile(o[:, 0:NT], weights("wc"), m, qcT, CH)
                    else:
                        taken(pe, "sv", NS - 1)
                        last = wide_tile(o[:, 0:NT], weights("wb"), m, bT, HPG)
                elif kind == "g":
                    br_, m = a
                    last = wide_tile(o[:, 0:NT], weights(f"g{br_}{m // 4}"), m % 4, hT)
                elif kind == "score":
                    n, (what, h, t) = a
                    if n >= 1:
                        pe.wait_ge(s_exp, n)
                    if what == "C":
                        mm(wide[0][:, 0:NM], qcT[:, h, t * P:(t + 1) * P], kcT[:, h, :]).then_inc(s_score, 1)
                    else:
                        pe.wait_ge(s_hank, 16)
                        nk = (t + 1) * P
                        for g in range(NG):
                            hh = g * HPG + h
                            r = slice(HD * (hh % 2), HD * (hh % 2) + HD)
                            so = wide[0][:, g * 256:g * 256 + nk]
                            mm(so, flip, hank[:, hh, 2 * P - nk:2 * P], True, False)
                            last = mm(so, qT[r, hh // 2, t * P:(t + 1) * P], kT[r, hh // 2, 0:nk], False, True)
                        last.then_inc(s_score, 1)
                elif kind == "turn":
                    n, (what, h, t) = a
                    pe.wait_ge(s_prob, n + 1)
                    if n >= 1:
                        pe.wait_ge(s_pt, n)
                    i = 0
                    for g in range(1 if what == "C" else NG):
                        for j in range(2 if what == "C" else t + 1):
                            last = turn(wide[1][:, i * P:(i + 1) * P], probs[n % 2][:, g * 256 + j * P:g * 256 + (j + 1) * P], P)
                            i += 1
                    last.then_inc(s_turned, 1)
                elif kind == "mix":
                    n, (what, h, t) = a
                    pe.wait_ge(s_pt, n + 1)
                    if n >= 1:
                        pe.wait_ge(s_mixout, n)
                    if what == "C":
                        for j in range(2):
                            last = mm(bank[3][:, 0:P], kvc[:, j, 512 + h * P:512 + (h + 1) * P], probs_t[n % 2][:, j * P:(j + 1) * P],
                                      j == 0, j == 1)
                    else:
                        nb = NG * (t + 1)
                        for i in range(nb):
                            g, j = i // (t + 1), i % (t + 1)
                            hh = g * HPG + h
                            last = mm(bank[3][0:HD, 0:P], v_tok[:, j, hh * HD:(hh + 1) * HD], probs_t[n % 2][:, i * P:(i + 1) * P],
                                      i == 0, i == nb - 1)
                    last.then_inc(s_mixed, 1)
                elif kind == "ssum":
                    pe.wait_ge(s_done["sexp"], 2)
                    last = mm(o[:, 0:NS * (NH + 2 * CH)], ones[:], samp[:])
                elif kind == "sv":
                    b, = a
                    pe.wait_ge(s_done["sprob"], 1)
                    pe.wait_ge(s_kvin[b % 2], 64 * (NS // 2 + b // 2 + 1))
                    pb = sB.rearrange("p (b h) -> p b h", b=NS)
                    pc = sC.rearrange("p (b t h) -> p b t h", b=NS, t=2)
                    for h in range(HPG):
                        for g in range(NG):
                            hh = g * HPG + h
                            mm(o[0:HD, h:h + 1], kv_b[b % 2][:, g, h * HD:(h + 1) * HD], pb[:, b, hh:hh + 1], g == 0, g == NG - 1)
                    for h in range(CH):
                        for j in range(2):
                            last = mm(o[:, HPG + h:HPG + h + 1], kv_c[b % 2][:, j, h * P:(h + 1) * P], pc[:, b, j, h:h + 1],
                                      j == 0, j == 1)
                elif kind == "wo":
                    t, n = a
                    pe.wait_ge(s_done["merged"], 3 * KD)
                    last = row_tile(o, merged, weights(f"o{n}"), t, 512)
                elif kind == "brow":
                    n, = a
                    pe.wait_ge(s_brow_in, 32)
                    for i in range(KD):
                        last = turn(o[:, i * E:(i + 1) * E], brow[:, (n * KD + i) * P:(n * KD + i + 1) * P], E)
                elif kind == "hT":
                    k, = a
                    pe.wait_ge(s_done["xr"], 1)
                    for t, (t0, tn) in enumerate(TILES):
                        last = turn(o[:, t0:t0 + tn], xr[0:tn, t, k * P:(k + 1) * P], tn)
                elif kind == "rt":
                    taken(pe, "hT", KD - 1)
                    pe.wait_ge(s_router_in, 32)
                    last = row_tile(o, merged, wr, a[0], E)
                elif kind == "pos":
                    pe.wait_ge(s_done["masks"], 1)
                    for t in range(3):
                        for u in range(t + 1):
                            mm(o[:, t * E:(t + 1) * E], before if u == t else ones[:], msk[:, u, :], u == 0, u == t)
                    for t in range(3):
                        last = mm(o[0:1, 3 * E:4 * E], ones[:, 0:1], msk[:, t, :], t == 0, t == 2)
                if kind in ROTATING:
                    last.then_inc(s_job, 1)

            for n in range(len(job) - 3, len(job)):
                pe.wait_ge(s_taken[n % 3], n // 3 + 1)
            h_gate, h_up, p_x, p_y = bank[0], bank[1], bank[2], bank[3]
            p_turn, p_s = wide[0], (wide[1][:, 0:512], wide[1][:, 512:1024])

            def gather(count):
                pe.wait_ge(s_p, count)
                for k in range(KD):
                    for t, (_, tn) in enumerate(TILES):
                        last = mm(p_x[:, k * SLOTS:(k + 1) * SLOTS], xr[0:tn, t, k * P:(k + 1) * P], sel_p[0:tn, t, :], t == 0, t == 2)
                last.then_inc(s_gath, 1)

            def turn_y(n33):
                pe.wait_ge(s_yT, n33 + 1)
                pe.sem_inc(s_carry, 1)
                for k in range(KD):
                    last = turn(p_turn[0:SLOTS, k * P:(k + 1) * P], yT[:, k, :], P)
                last.then_inc(s_yturn, 1)

            def scatter(n33):
                pe.wait_ge(s_ytok, n33 + 1)
                pe.wait_ge(s_gT, n33 + 1)
                for c in range(KD):
                    if c >= 2:
                        pe.wait_ge(s_acc, n33 * KD + (c - 1))
                    mm(p_s[(c + 1) % 2][:, 0:NT], y_tok[:, c * P:(c + 1) * P], gT).then_inc(s_scat, 1)

            def one_pass(b):
                gather(b * (E + 1) + 1)
                with pe.Fori(0, E) as i:
                    n33 = b * (E + 1) + i
                    n32 = b * E + i
                    pe.wait_ge(s_xg, n33 + 1)
                    for k in range(KD):
                        w = chunk_view(k)
                        pe.wait_ge(s_chunk_in[chunk_slot(k)], n32 * 16 + 16)
                        for m in range(GU):
                            ho = (h_gate, h_up)[m // KD][:, (m % KD) * SLOTS:(m % KD + 1) * SLOTS]
                            last = mm(ho, w[:, m * P:(m + 1) * P], xg[:, k, :], k == 0 and m % KD == 0, k == KD - 1,
                                      skip_group_check=True)
                            if m == GU - 1:
                                last.then_inc(s_chunk_used, 1)
                    turn_y(n33)
                    gather(n33 + 2)
                    scatter(n33)
                    pe.wait_ge(s_acc, n33 * KD + KD)
                    pe.wait_ge(s_pg, n32 + 1)
                    pe.sem_inc(s_carry, 1)
                    for t, (t0, tn) in enumerate(TILES):
                        last = turn(p_s[0][0:SLOTS, t0:t0 + tn], sel_g[0:tn, t, :], tn)
                    last.then_inc(s_gturn, 1)
                    pe.wait_ge(s_actv, n32 + 1)
                    for k in range(KD):
                        c = KD + k // 2
                        if k % 2 == 0:
                            pe.wait_ge(s_chunk_in[chunk_slot(c)], n32 * 16 + 16)
                        w = chunk_view(c).rearrange("p (j c) -> p j c", j=2)[:, k % 2, :]
                        for m in range(KD):
                            last = mm(p_y[:, m * SLOTS:(m + 1) * SLOTS], w[:, m * P:(m + 1) * P], actv[:, k, :],
                                      k == 0 and m == 0, k == KD - 1, skip_group_check=True)
                        if k % 2:
                            last.then_inc(s_chunk_used, 1)
                turn_y(b * (E + 1) + E)
                scatter(b * (E + 1) + E)

            one_pass(0)
            flag = pe.value_load(over[0:1, 0:1], min_val=0, max_val=NT)
            with pe.If(flag > SLOTS):
                with pe.Fori(1, PASSES) as ps:
                    one_pass(ps)
            pe.wait_ge(s_accout, 1)
            for t, (t0, tn) in enumerate(TILES):
                w = wide[t % 2]
                if t == 2:
                    pe.wait_ge(s_finT, 1)
                for k in range(KD):
                    last = turn(w[0:tn, k * P:(k + 1) * P], acc[:, k, t0:t0 + tn], P)
                last.then_inc(s_finj, 1)

        @block.vector
        def _(dve):
            done = [0]

            def seq(ins):
                done[0] += 1
                ins.then_inc(s_dve, 1)
                dve.wait_ge(s_dve, done[0])

            def rms_scale(r, n, count):
                dve.wait_ge(s_ss, count)
                nc.vector.tensor_scalar(r, r, 1.0 / n, EPS, ALU.mult, ALU.add).then_inc(s_ms, 1)

            V = nc.vector
            V.memset(ones[:], 1.0).then_inc(s_done["ones"], 1)
            seq(V.memset(stat[:], 1.0))
            V.memset(rel[REL_BUCKETS:REL_BUCKETS + 1, :], 1.0).then_inc(s_done["ones"], 1)
            rms_scale(stat[:, 0:2], D, 2)
            dve.wait_ge(s_rt, 1)
            seq(V.reciprocal(stat[:, 0:2], stat[:, 0:2]))
            for t in range(2):
                ins = V.tensor_scalar(mem_tok[:, t, :], mem_tok[:, t, :], stat[:, t:t + 1], None, ALU.mult)
                if t == 0:
                    seq(ins)
            ins.then_inc(s_done["memn"], 1)
            rms_scale(stat[:, 2:5], D, 5)
            dve.wait_ge(s_rt, 2)
            seq(V.reciprocal(stat[:, 2:5], stat[:, 2:5]))
            for t, (_, tn) in enumerate(TILES):
                ins = V.tensor_scalar(x1[0:tn, t, :], x1[0:tn, t, :], stat[0:tn, 2 + t:3 + t], None, ALU.mult)
                if t < 2:
                    seq(ins)
            ins.then_inc(s_done["xn"], 1)

            for s in steps:
                kind, a = s[0], s[1:]
                if kind in ROTATING:
                    n = job[s]
                    o = bank[n % 3]
                    free = s_taken[n % 3]

                    def ready(n=n):
                        dve.wait_ge(s_job, n + 1)

                    def own(n=n):
                        dve.wait_ge(s_taken[n % 3], n // 3 + 1)
                if kind == "vec":
                    ready()
                    V.tensor_copy(vec[:], o[:, 0:3 * KD]).then_inc(free, 1)
                    own()
                elif kind == "wsp":
                    ready()
                    V.tensor_tensor(wspT[:], o[:].rearrange("p (g i) -> p g i", g=AG),
                                        triu.unsqueeze(1).to_broadcast([P, AG, P]), ALU.mult).then_inc(free, 1)
                elif kind == "sbias":
                    ready()
                    V.tensor_copy(sbias[:], o[:, 0:2 * NH]).then_inc(free, 1)
                    own()
                elif kind == "memT":
                    k, = a
                    ready()
                    V.tensor_scalar(memT[:, k, :], o[:, 0:NM], g_mem[:, k:k + 1], None, ALU.mult).then_inc(free, 1)
                elif kind == "xT":
                    k, = a
                    ready()
                    V.tensor_scalar(hT[:, k, :], o[:, 0:NT], g_mix[:, k:k + 1], None, ALU.mult).then_inc(free, 1)
                elif kind == "q":
                    ready()
                    V.tensor_scalar(qT[:, a[0], :], o[:, 0:NT], B_SCALE, None, ALU.mult).then_inc(free, 1)
                elif kind == "kt":
                    t, n2 = a
                    tn = TILES[t][1]
                    ready()
                    V.tensor_copy(k_tok[0:tn, t, n2 * 384:(n2 + 1) * 384], o[0:tn, 0:384]).then_inc(free, 1)
                elif kind == "qc":
                    ready()
                    V.tensor_copy(qcT[:, a[0], :], o[:, 0:NT]).then_inc(free, 1)
                elif kind in ("qs", "qcs"):
                    c, w = (a[0] * 384, 384) if kind == "qs" else (BW, 512)
                    ready()
                    V.tensor_copy(qs[:, c:c + w], o[0:NS, 0:w]).then_inc(free, 1)
                    own()
                    if kind == "qcs":
                        seq(V.tensor_tensor(slf, qs[:, 0:BW], k_tok[0:NS, 2, :], ALU.mult))
                        seq(V.tensor_reduce(slog[:], slf.rearrange("p (h c) -> p h c", c=HD), AX.X, ALU.add))
                        seq(V.tensor_tensor(slog[:], slog[:], sbias[0:NS, NH:2 * NH], ALU.add))
                        V.tensor_tensor(sdiag[:], ident[0:NS, 0:NS].unsqueeze(2).to_broadcast([NS, NS, NH]),
                                        slog[:].unsqueeze(1).to_broadcast([NS, NS, NH]), ALU.mult).then_inc(s_done["sdiag"], 1)
                elif kind == "vts":
                    ready()
                    V.tensor_copy(vts[:], o[0:HD, 0:NH * NS].rearrange("p (h b) -> p h b", h=NH)).then_inc(free, 1)
                    own()
                elif kind == "selfb":
                    ready()
                    V.tensor_copy(sself[:], o[:, 0:NS * NH]).then_inc(free, 1)
                    own()
                elif kind == "sk":
                    b, n2 = a
                    if n2 == 0:
                        dve.wait_ge(s_kvin[b % 2], 64 * (b // 2 + 1))
                    ready()
                    kk = kv_b[b % 2].rearrange("p g c -> p (g c)")[:, n2 * 384:(n2 + 1) * 384]
                    V.tensor_tensor(prod[:, 0:384], kk, o[:, 0:384], ALU.mult).then_inc(free, 1)
                    own()
                    seq(V.tensor_reduce(sB[:, b * NH + 6 * n2:b * NH + 6 * n2 + 6], prod[:, 0:384].rearrange("p (h c) -> p h c", c=HD),
                                        AX.X, ALU.add))
                elif kind == "skc":
                    b, = a
                    ready()
                    V.tensor_tensor(prod.rearrange("p (t c) -> p t c", t=2), kv_c[b % 2], o[:].unsqueeze(1).to_broadcast([P, 2, 512]),
                                        ALU.mult).then_inc(free, 1)
                    own()
                    dve.sem_inc(s_kv_used, 1)
                    seq(V.tensor_reduce(sC[:, b * 8:(b + 1) * 8], prod.rearrange("p (h c) -> p h c", c=CD), AX.X, ALU.add))
                elif kind == "norm_v":
                    taken(dve, "zv", 2)
                    for t, (_, tn) in enumerate(TILES):
                        seq(V.bn_stats(bn[0:tn, t, :], va[0:tn, t, :]))
                        seq(V.bn_aggr(bna[0:tn, t, :], bn[0:tn, t, :]))
                        seq(V.tensor_scalar(stat[0:tn, 8 + t:9 + t], bna[0:tn, t, 1:2], EPS, None, ALU.add))
                    dve.sem_inc(s_ms, 1)
                    dve.wait_ge(s_rt, 3)
                    seq(V.reciprocal(stat[:, 8:11], stat[:, 8:11]))
                    dve.wait_ge(s_lnw, 32)
                    for t, (_, tn) in enumerate(TILES):
                        v = va[0:tn, t, :]
                        seq(V.tensor_scalar(v, v, bna[0:tn, t, 0:1], stat[0:tn, 8 + t:9 + t], ALU.subtract, ALU.mult))
                        seq(V.tensor_tensor(v, v, lnw[0:tn, 0, :], ALU.mult))
                        seq(V.tensor_tensor(v, v, lnw[0:tn, 1, :], ALU.add))
                    dve.sem_inc(s_done["va"], 1)
                elif kind == "vat":
                    dve.wait_ge(s_bsp, 16)
                    dve.wait_ge(s_w00, 16)
                    taken(dve, "zu", AG - 1)
                    ready()
                    t3 = tmp[0][:, 0:AG * NS].rearrange("p (g b) -> p g b", g=AG)
                    V.tensor_tensor(t3, o[:, 0:AG * NS].rearrange("p (g b) -> p g b", g=AG),
                                        w00[:].unsqueeze(2).to_broadcast([P, AG, NS]), ALU.mult).then_inc(free, 1)
                    own()
                    seq(V.tensor_tensor(t3, t3, bsp[:, :, 0:1].to_broadcast([P, AG, NS]), ALU.add))
                    V.tensor_tensor(uT[:, :, SEQ:NT], uT[:, :, SEQ:NT], t3, ALU.mult).then_inc(s_done["aT"], 1)
                elif kind == "sp":
                    g, = a
                    ready()
                    t2 = tmp[1][:, 0:SEQ].rearrange("p (t i) -> p t i", t=2)
                    V.tensor_tensor(t2, o[:, 0:SEQ].rearrange("p (t i) -> p t i", t=2),
                                        bsp[:, g, :].unsqueeze(1).to_broadcast([P, 2, P]), ALU.add).then_inc(free, 1)
                    own()
                    seq(V.tensor_tensor(uT[:, g, 0:SEQ], uT[:, g, 0:SEQ], tmp[1][:, 0:SEQ], ALU.mult))
                    dve.sem_inc(s_done["aT"], 1)
                elif kind == "slog":
                    b3 = sB.rearrange("p (b h) -> p b h", b=NS)
                    seq(V.tensor_scalar(sC, sC, C_SCALE, None, ALU.mult))
                    seq(V.tensor_tensor(b3, b3, sbias[:, 0:NH].unsqueeze(1).to_broadcast([P, NS, NH]), ALU.add))
                    dve.sem_inc(s_done["lgs"], 1)
                    dve.wait_ge(s_done["parmax"], 1)
                    mB = smax[:, 0:NS * NH]
                    seq(V.tensor_tensor(mB, mB, sself[:], ALU.max))
                    m4 = mB.rearrange("p (b g h) -> p b h g", b=NS, g=NG)
                    m5 = smax[:, NS * NH:].rearrange("p (b t h) -> p b h t", b=NS, t=2)
                    top3 = stop[:, 0:NS * HPG].rearrange("p (b h) -> p b h", b=NS)
                    top4 = stop[:, NS * HPG:].rearrange("p (b h) -> p b h", b=NS)
                    seq(V.tensor_reduce(top3, m4, AX.X, ALU.max))
                    seq(V.tensor_reduce(top4, m5, AX.X, ALU.max))
                    s4 = sB.rearrange("p (b g h) -> p b g h", b=NS, g=NG)
                    f4 = sself[:].rearrange("p (b g h) -> p b g h", b=NS, g=NG)
                    c4 = sC.rearrange("p (b t h) -> p b t h", b=NS, t=2)
                    seq(V.tensor_tensor(s4, s4, top3.unsqueeze(2).to_broadcast([P, NS, NG, HPG]), ALU.subtract))
                    seq(V.tensor_tensor(f4, f4, top3.unsqueeze(2).to_broadcast([P, NS, NG, HPG]), ALU.subtract))
                    seq(V.tensor_tensor(c4, c4, top4.unsqueeze(2).to_broadcast([P, NS, 2, CH]), ALU.subtract))
                    dve.sem_inc(s_done["lgs"], 1)
                elif kind == "ssum":
                    ready()
                    seq(V.tensor_tensor(smax[:, 0:NS * NH], o[:, 0:NS * NH], sself[:], ALU.add))
                    V.tensor_copy(smax[:, NS * NH:], o[:, NS * NH:NS * (NH + 2 * CH)]).then_inc(free, 1)
                    own()
                    t3 = stot[:, 0:NS * HPG].rearrange("p (b h) -> p b h", b=NS)
                    t4 = stot[:, NS * HPG:].rearrange("p (b h) -> p b h", b=NS)
                    seq(V.tensor_reduce(t3, smax[:, 0:NS * NH].rearrange("p (b g h) -> p b h g", b=NS, g=NG), AX.X, ALU.add))
                    seq(V.tensor_reduce(t4, smax[:, NS * NH:].rearrange("p (b t h) -> p b h t", b=NS, t=2), AX.X, ALU.add))
                    seq(V.reciprocal(stot[:], stot[:]))
                    s4 = sB.rearrange("p (b g h) -> p b g h", b=NS, g=NG)
                    f4 = sself[:].rearrange("p (b g h) -> p b g h", b=NS, g=NG)
                    c4 = sC.rearrange("p (b t h) -> p b t h", b=NS, t=2)
                    seq(V.tensor_tensor(s4, s4, t3.unsqueeze(2).to_broadcast([P, NS, NG, HPG]), ALU.mult))
                    seq(V.tensor_tensor(f4, f4, t3.unsqueeze(2).to_broadcast([P, NS, NG, HPG]), ALU.mult))
                    seq(V.tensor_tensor(c4, c4, t4.unsqueeze(2).to_broadcast([P, NS, 2, CH]), ALU.mult))
                    dve.sem_inc(s_done["sprob"], 1)
                    pf = sself[0:HD, :].rearrange("p (b h) -> p h b", b=NS)
                    seq(V.tensor_tensor(vts[:], vts[:], pf, ALU.mult))
                    seq(V.tensor_reduce(vself[:], vts[:].rearrange("p (g h) b -> p h b g", g=NG), AX.X, ALU.add))
                elif kind == "sv":
                    b, = a
                    ready()
                    seq(V.tensor_tensor(bT[:, :, SEQ + b:SEQ + b + 1], o[0:HD, 0:HPG].unsqueeze(2), vself[:, :, b:b + 1], ALU.add))
                    V.tensor_copy(qcT[:, :, SEQ + b:SEQ + b + 1], o[:, HPG:HPG + CH].unsqueeze(2)).then_inc(free, 1)
                    dve.sem_inc(s_kv_used, 1)
                elif kind == "score":
                    n2, (what, h, t) = a
                    dve.wait_ge(s_score, n2 + 1)
                    m = stat[:, 16 + n2 % 2:17 + n2 % 2]
                    if what == "C":
                        seq(V.tensor_reduce(m, wide[0][:, 0:NM], AX.X, ALU.max))
                        V.tensor_scalar(m, m, -C_SCALE, None, ALU.mult).then_inc(s_max, 1)
                    else:
                        nk = (t + 1) * P
                        src = wide[0][:, 0:768].rearrange("p (g k) -> p g k", g=NG)[:, :, 0:nk]
                        seq(V.tensor_reduce(m, src, AX.XY, ALU.max))
                        V.tensor_scalar(m, m, -1.0, None, ALU.mult).then_inc(s_max, 1)
                    dve.wait_ge(s_exp, n2 + 1)
                    r = stat[:, 18 + n2 % 2:19 + n2 % 2]
                    seq(V.reciprocal(r, r))
                    if what == "C":
                        pv = probs[n2 % 2][:, 0:NM]
                    else:
                        pv = probs[n2 % 2].rearrange("p (g k) -> p g k", g=NG)[:, :, 0:(t + 1) * P]
                    V.tensor_scalar(pv, pv, r, None, ALU.mult).then_inc(s_prob, 1)
                elif kind == "mix":
                    n2, (what, h, t) = a
                    dve.wait_ge(s_mixed, n2 + 1)
                    ts = slice(t * P, (t + 1) * P)
                    if what == "C":
                        V.tensor_copy(qcT[:, h, ts], bank[3][:, 0:P]).then_inc(s_mixout, 1)
                    else:
                        V.tensor_copy(bT[:, h, ts], bank[3][0:HD, 0:P]).then_inc(s_mixout, 1)
                elif kind == "g":
                    br_, m = a
                    i = "acb".index(br_) * KD + m
                    n = job[("p", br_, m)]
                    o = bank[n % 3]
                    taken(dve, *s)
                    V.scalar_tensor_tensor(tmp[i % 2], th[i % 2][:], 1.0, o[:, 0:NT], ALU.add, ALU.mult).then_inc(s_taken[n % 3], 1)
                    dve.wait_ge(s_taken[n % 3], n // 3 + 1)
                    if br_ == "a":
                        if m == 0:
                            taken(dve, "kct", 1)
                        V.tensor_scalar(merged[:, m, :], tmp[i % 2], 0.5, None, ALU.mult).then_inc(s_done["merged"], 1)
                    else:
                        seq(V.scalar_tensor_tensor(merged[:, m, :], tmp[i % 2], 0.5, merged[:, m, :], ALU.mult, ALU.add))
                        dve.sem_inc(s_done["merged"], 1)
                elif kind == "wo":
                    t, n2 = a
                    tn = TILES[t][1]
                    dve.wait_ge(s_xagain, 32)
                    ready()
                    xs = x1[0:tn, t, n2 * 512:(n2 + 1) * 512]
                    V.tensor_tensor(xs, xs, o[0:tn, :], ALU.add).then_inc(free, 1)
                elif kind == "norm_f":
                    rms_scale(stat[:, 24:27], D, 8)
                    dve.wait_ge(s_rt, 4)
                    seq(V.reciprocal(stat[:, 24:27], stat[:, 24:27]))
                    dve.wait_ge(s_kvout, 16 * 12)
                    for t, (_, tn) in enumerate(TILES):
                        seq(V.tensor_scalar(xr[0:tn, t, :], x1[0:tn, t, :], stat[0:tn, 24 + t:25 + t], None, ALU.mult))
                    dve.sem_inc(s_done["xr"], 1)
                    dve.wait_ge(s_vaout, 16)
                    seq(V.memset(small[:, 0:880], 0.0))
                elif kind == "brow":
                    n2, = a
                    ready()
                    V.tensor_copy(bexp[:, n2 * KD:(n2 + 1) * KD, :], o[:, 0:KD * E].rearrange("p (k e) -> p k e", k=KD)).then_inc(free, 1)
                    own()
                elif kind == "hT":
                    k, = a
                    ready()
                    V.tensor_scalar(merged[:, k, :], o[:, 0:NT], g_ffn[:, k:k + 1], None, ALU.mult).then_inc(free, 1)
                elif kind == "rt":
                    t, = a
                    tn = TILES[t][1]
                    ready()
                    dve.wait_ge(s_router_in, 32)
                    V.tensor_tensor(lg[0:tn, t, :], o[0:tn, 0:E], br[0:tn, :], ALU.add).then_inc(free, 1)
                    own()
                elif kind == "top":
                    for t in range(3):
                        seq(V.max(mx8[:, t, :], lg[:, t, :]))
                        seq(V.max_index(idx[:, t, :], mx8[:, t, :], lg[:, t, :]))
                    seq(V.tensor_copy(idf, idx[:]))
                    V.tensor_tensor(gk, mx8[:, :, 0:TOPK], mx8[:, :, 0:1].to_broadcast([P, 3, TOPK]), ALU.subtract).then_inc(s_tmax, 1)
                    dve.wait_ge(s_texp, 1)
                    seq(V.tensor_reduce(gsum, gk, AX.X, ALU.add))
                    seq(V.reciprocal(gsum, gsum))
                    seq(V.tensor_tensor(gk, gk, gsum.unsqueeze(2).to_broadcast([P, 3, TOPK]), ALU.mult))
                    dve.wait_ge(s_iota, 1)
                    seq(V.tensor_tensor(eq, iota[:, 0:E].unsqueeze(1).unsqueeze(3).to_broadcast([P, 3, E, TOPK]),
                                        idf[:, :, 0:TOPK].unsqueeze(2).to_broadcast([P, 3, E, TOPK]), ALU.is_equal))
                    seq(V.tensor_reduce(msk, eq, AX.X, ALU.add))
                    seq(V.tensor_tensor(msk, msk, valid.unsqueeze(2).to_broadcast([P, 3, E]), ALU.mult))
                    dve.sem_inc(s_done["masks"], 1)
                    seq(V.tensor_tensor(eq, eq, gk.unsqueeze(2).to_broadcast([P, 3, E, TOPK]), ALU.mult))
                    seq(V.tensor_reduce(gw, eq, AX.X, ALU.add))
                elif kind == "pos":
                    ready()
                    seq(V.memset(posm, -1.0))
                    seq(V.scalar_tensor_tensor(posm[:, :, 0:E], o[:, 0:3 * E].rearrange("p (t e) -> p t e", t=3), 1.0, msk, ALU.add, ALU.mult))
                    seq(V.tensor_scalar(posm[:, :, 0:E], posm[:, :, 0:E], -1.0, None, ALU.add))
                    seq(V.tensor_reduce(most, o[0:1, 3 * E:4 * E], AX.X, ALU.max))
                    V.tensor_copy(over[:], most).then_inc(free, 1)
                    own()
                    dve.sem_inc(s_done["posm"], 1)

            V.memset(acc[:], 0.0).then_inc(s_dve, 1)
            done[0] += 1
            dve.wait_ge(s_dve, done[0])
            STEPS = 9

            def select(b, e):
                return V.tensor_tensor(sel_p, iota[:, bass.ds(b * SLOTS, SLOTS)].unsqueeze(1).to_broadcast([P, 3, SLOTS]) if not isinstance(b, int)
                                       else iota[:, b * SLOTS:(b + 1) * SLOTS].unsqueeze(1).to_broadcast([P, 3, SLOTS]),
                                       posm[:, :, bass.ds(e, 1)].to_broadcast([P, 3, SLOTS]) if not isinstance(e, int)
                                       else posm[:, :, e:e + 1].to_broadcast([P, 3, SLOTS]), ALU.is_equal)

            def take_x(n33):
                dve.wait_ge(s_gath, n33 + 1)
                V.tensor_tensor(xg, bank[2][:].rearrange("p (k s) -> p k s", k=KD), g_ffn.unsqueeze(2).to_broadcast([P, KD, SLOTS]),
                                ALU.mult).then_inc(s_xg, 1)

            def add_up(n33):
                for c in range(KD):
                    dve.wait_ge(s_scat, n33 * KD + (c + 1))
                    V.tensor_tensor(acc[:, c, :], wide[1][:, ((c + 1) % 2) * 512:((c + 1) % 2) * 512 + NT], acc[:, c, :],
                                    ALU.add).then_inc(s_acc, 1)

            def one_pass(b):
                V.memset(yT, 0.0).then_inc(s_yT, 1)
                V.memset(gT, 0.0).then_inc(s_gT, 1)
                select(b, 0).then_inc(s_p, 1)
                take_x(b * (E + 1))
                with dve.Fori(0, E) as i:
                    n33 = b * (E + 1) + i
                    n32 = b * E + i
                    step = [0]

                    def link(ins):
                        step[0] += 1
                        ins.then_inc(s_loop, 1)
                        dve.wait_ge(s_loop, n32 * STEPS + step[0])

                    V.tensor_tensor(sel_g, sel_p, gw[:, :, bass.ds(i, 1)].to_broadcast([P, 3, SLOTS]), ALU.mult).then_inc(s_pg, 1)
                    dve.wait_ge(s_pg, n32 + 1)
                    select(b, i + 1).then_inc(s_p, 1)
                    dve.wait_ge(s_chunk_used, n32 * CHUNKS + KD)
                    link(V.tensor_tensor(gate, bank[0][:].rearrange("p (k s) -> p k s", k=KD),
                                         bexp[:, 0:KD, bass.ds(i, 1)].to_broadcast([P, KD, SLOTS]), ALU.add))
                    V.tensor_scalar(gate, gate, LIMIT, None, ALU.min).then_inc(s_gate, 1)
                    link(V.tensor_tensor(up, bank[1][:].rearrange("p (k s) -> p k s", k=KD),
                                         bexp[:, KD:2 * KD, bass.ds(i, 1)].to_broadcast([P, KD, SLOTS]), ALU.add))
                    link(V.tensor_scalar(up, up, LIMIT, -LIMIT, ALU.min, ALU.max))
                    dve.wait_ge(s_gate, n32 + 1)
                    link(V.scalar_tensor_tensor(up, up, 1.0, gate, ALU.add, ALU.mult))
                    dve.wait_ge(s_sig, n32 + 1)
                    V.tensor_tensor(actv, up, sig, ALU.mult).then_inc(s_actv, 1)
                    take_x(n33 + 1)
                    add_up(n33)
                    dve.wait_ge(s_chunk_used, n32 * CHUNKS + CHUNKS)
                    V.tensor_tensor(yT, bank[3][:].rearrange("p (k s) -> p k s", k=KD),
                                    bexp[:, 2 * KD:3 * KD, bass.ds(i, 1)].to_broadcast([P, KD, SLOTS]), ALU.add).then_inc(s_yT, 1)
                    while step[0] < STEPS:
                        step[0] += 1
                        dve.sem_inc(s_loop, 1)
                add_up(b * (E + 1) + E)
                dve.wait_ge(s_acc, b * ((E + 1) * KD) + (E + 1) * KD)

            one_pass(0)
            flag = dve.value_load(over[0:1, 0:1], min_val=0, max_val=NT)
            with dve.If(flag > SLOTS):
                with dve.Fori(1, PASSES) as ps:
                    one_pass(ps)
            dve.sem_inc(s_accout, 1)
            for t, (_, tn) in enumerate(TILES):
                dve.wait_ge(s_finj, t + 1)
                V.tensor_tensor(x1[0:tn, t, :], x1[0:tn, t, :], wide[t % 2][0:tn, :], ALU.add).then_inc(s_finT, 1)
            rms_scale(stat[:, 28:31], D, 11)
            dve.wait_ge(s_rt, 5)
            seq(V.reciprocal(stat[:, 28:31], stat[:, 28:31]))
            dve.wait_ge(s_gfin_in, 16)
            for t, (_, tn) in enumerate(TILES):
                V.scalar_tensor_tensor(x1[0:tn, t, :], x1[0:tn, t, :], stat[0:tn, 28 + t:29 + t], gfin[0:tn, :], ALU.mult,
                                       ALU.mult).then_inc(s_fin, 1)

        @block.scalar
        def _(act):
            A = nc.scalar
            done = [0]

            def seq(ins):
                done[0] += 1
                ins.then_inc(s_act, 1)
                act.wait_ge(s_act, done[0])

            with nc.allow_non_contiguous_dma(reason="small vectors"):
                act.dma_start(sq[:], C["square"]).then_inc(s_sq, 16)
                for n, name in enumerate(("norm_mix", "norm_mem", "norm_ffn")):
                    act.dma_start(vecr[n * KD:(n + 1) * KD, :], I[name][0].rearrange("(k p) -> k p", p=P)).then_inc(s_vecr, 16)
                act.dma_start(wsp[:], I["w_spatial"][0].rearrange("g i j -> i g j")).then_inc(s_wsp, 16)
                act.dma_start(rel[0:REL_BUCKETS, :], I["rel_bias"]).then_inc(s_rel, 16)
                act.dma_start(selh.rearrange("p g x -> p (g x)"), C["hankel"]).then_inc(s_rel, 16)
                act.dma_start(sels.rearrange("p g x -> p (g x)"), C["sample"]).then_inc(s_sels, 16)
                act.dma_start(lnw[:, 0, :], I["ln_v_g"].to_broadcast([P, 512])).then_inc(s_lnw, 16)
                act.dma_start(lnw[:, 1, :], I["ln_v_b"].to_broadcast([P, 512])).then_inc(s_lnw, 16)
                act.dma_start(bsp[:].rearrange("p g i -> p (g i)"),
                              I["b_spatial"].rearrange("d g i -> d (g i)").to_broadcast([P, AG * P])).then_inc(s_bsp, 16)
                act.dma_start(w00[:], I["w_spatial"][:, :, 0, 0].to_broadcast([P, AG])).then_inc(s_w00, 16)
                act.dma_start(wr[:], I["w_router"][0].rearrange("(k p) e -> p k e", p=P)).then_inc(s_router_in, 16)
                act.dma_start(br[:], I["b_router"].to_broadcast([P, E])).then_inc(s_router_in, 16)

            def squares(dst, src, junk):
                A.activation(junk, src, ACT.Square, accum_out=dst).then_inc(s_ss, 1)

            junk = merged[:, :, :].rearrange("p a b -> p (a b)")
            act.wait_ge(s_dve, 1)
            act.wait_ge(s_mem_in, 16)
            for t in range(2):
                squares(stat[:, t:t + 1], mem_tok[:, t, :], junk[:, t * D:(t + 1) * D])
            act.wait_ge(s_ms, 1)
            A.activation(stat[:, 0:2], stat[:, 0:2], ACT.Sqrt).then_inc(s_rt, 1)
            act.wait_ge(s_x_in, 32)
            junk2 = qk[:, :, :].rearrange("p a b -> p (a b)")
            for t, (_, tn) in enumerate(TILES):
                squares(stat[0:tn, 2 + t:3 + t], x1[0:tn, t, :], junk2[0:tn, t * D:(t + 1) * D])
            act.wait_ge(s_ms, 2)
            A.activation(stat[:, 2:5], stat[:, 2:5], ACT.Sqrt).then_inc(s_rt, 1)

            for s in steps:
                kind, a = s[0], s[1:]
                if kind in ROTATING:
                    n = job[s]
                    o = bank[n % 3]
                    free = s_taken[n % 3]

                    def take(out, in_, name, n=n, free=free):
                        act.wait_ge(s_job, n + 1)
                        A.copy(out, in_).then_inc(free, 1)
                if kind == "rel":
                    take(hrow[:, a[0], :], o[0:HPG, 0:HANK], "hrow")
                elif kind == "kc":
                    take(kcT[:, a[0], :], o[:, 0:NM], "kcT")
                elif kind == "vc":
                    take(kvc[:, a[0], 512:1024], o[:], "kvc")
                elif kind == "kct":
                    take(kvc[:, a[0], 0:512], o[:], "kvc")
                elif kind == "k":
                    take(kT[:, a[0], :], o[:, 0:NT], "k")
                elif kind == "v":
                    t, n2 = a
                    tn, w = TILES[t][1], (512, 256)[n2]
                    take(v_tok[0:tn, t, n2 * 512:n2 * 512 + w], o[0:tn, 0:w], "v")
                elif kind == "zv":
                    t, = a
                    tn = TILES[t][1]
                    act.wait_ge(s_job, n + 1)
                    A.activation(va[0:tn, t, :], o[0:tn, :], ACT.Gelu_apprx_tanh).then_inc(free, 1)
                elif kind == "zu":
                    act.wait_ge(s_job, n + 1)
                    A.activation(uT[:, a[0], :], o[:, 0:NT], ACT.Gelu_apprx_tanh).then_inc(free, 1)
                elif kind == "norm_v":
                    act.wait_ge(s_ms, 3)
                    A.activation(stat[:, 8:11], stat[:, 8:11], ACT.Sqrt).then_inc(s_rt, 1)
                elif kind == "slog":
                    act.wait_ge(s_done["lgs"], 2)
                    A.activation(samp[:], samp[:], ACT.Exp).then_inc(s_done["sexp"], 1)
                    A.activation(sself[:], sself[:], ACT.Exp).then_inc(s_done["sexp"], 1)
                elif kind == "score":
                    n2, (what, h, t) = a
                    act.wait_ge(s_max, n2 + 1)
                    m, r = stat[:, 16 + n2 % 2:17 + n2 % 2], stat[:, 18 + n2 % 2:19 + n2 % 2]
                    if n2 >= 2:
                        act.wait_ge(s_turned, n2 - 1)
                    if what == "C":
                        A.activation(probs[n2 % 2][:, 0:NM], wide[0][:, 0:NM], ACT.Exp, bias=m, scale=C_SCALE,
                                     accum_out=r).then_inc(s_exp, 1)
                    else:
                        nk = (t + 1) * P
                        A.activation(probs[n2 % 2].rearrange("p (g k) -> p g k", g=NG)[:, :, 0:nk],
                                     wide[0][:, 0:768].rearrange("p (g k) -> p g k", g=NG)[:, :, 0:nk], ACT.Exp, bias=m,
                                     accum_out=r).then_inc(s_exp, 1)
                elif kind == "turn":
                    n2, (what, h, t) = a
                    w = 2 * P if what == "C" else NG * (t + 1) * P
                    act.wait_ge(s_turned, n2 + 1)
                    if n2 >= 2:
                        act.wait_ge(s_mixed, n2 - 1)
                    A.copy(probs_t[n2 % 2][:, 0:w], wide[1][:, 0:w]).then_inc(s_pt, 1)
                elif kind == "g":
                    br_, m = a
                    i = "acb".index(br_) * KD + m
                    act.wait_ge(s_job, n + 1)
                    if i >= 2:
                        act.wait_ge(s_done["merged"], i - 1)
                    A.activation(th[i % 2][:], o[:, 0:NT], ACT.Tanh, scale=0.5).then_inc(free, 1)
                elif kind == "norm_f":
                    taken(act, "wo", 2, 1)
                    for t, (_, tn) in enumerate(TILES):
                        squares(stat[0:tn, 24 + t:25 + t], x1[0:tn, t, :], junk[0:tn, 0:D] if t == 0 else moe[0:tn, (t - 1) * D:t * D])
                    act.wait_ge(s_ms, 4)
                    A.activation(stat[:, 24:27], stat[:, 24:27], ACT.Sqrt).then_inc(s_rt, 1)
                    act.wait_ge(s_done["xr"], 1)
                    act.dma_start(gfin, I["norm_final"].rearrange("(a d) -> a d", a=1).to_broadcast([P, D])).then_inc(s_gfin_in, 16)
                elif kind == "top":
                    act.wait_ge(s_tmax, 1)
                    A.activation(gk, gk, ACT.Exp).then_inc(s_texp, 1)

            def take_y(n33):
                act.wait_ge(s_yturn, n33 + 1)
                A.copy(y_tok, wide[0][0:SLOTS, :]).then_inc(s_ytok, 1)

            def one_pass(b):
                with act.Fori(0, E) as i:
                    n33 = b * (E + 1) + i
                    n32 = b * E + i
                    act.wait_ge(s_gate, n32 + 1)
                    A.activation(sig, gate, ACT.Sigmoid, scale=ALPHA).then_inc(s_sig, 1)
                    take_y(n33)
                    act.wait_ge(s_gturn, n32 + 1)
                    A.copy(gT, wide[1][0:SLOTS, 0:NT]).then_inc(s_gT, 1)
                take_y(b * (E + 1) + E)

            one_pass(0)
            flag = act.value_load(over[0:1, 0:1], min_val=0, max_val=NT)
            with act.If(flag > SLOTS):
                with act.Fori(1, PASSES) as ps:
                    one_pass(ps)
            for t, (_, tn) in enumerate(TILES):
                act.wait_ge(s_finT, t + 1)
                squares(stat[0:tn, 28 + t:29 + t], x1[0:tn, t, :], xr[0:tn, t, :])
            act.wait_ge(s_ms, 5)
            A.activation(stat[:, 28:31], stat[:, 28:31], ACT.Sqrt).then_inc(s_rt, 1)


_INS = ["x_prompt", "x_sample", "cache_win0_kv", "cache_win1_kv", "cache_win2_kv", "cache_mem_kv", "mem_prompt", "rel_bias", "norm_mix",
        "norm_mem", "w_in", "ln_v_g", "ln_v_b", "w_spatial", "b_spatial", "w_mem_kv", "w_branch_a", "w_branch_b", "w_branch_c", "w_out",
        "norm_ffn", "w_router", "b_router", "w_gate_up", "b_gate_up", "w_down", "b_down", "norm_final"]
_OUTS = [(1, SEQ, D), (NS, 1, D), (1, 1, 128, 2, HPG, HD), (1, 1, 256, 2, HPG, HD), (1, 1, 256, 2, HPG, HD), (1, 1, NM, 2, CH, CD),
         (1, NS, 128, 2, HPG, HD), (1, NS, 512, 2, HPG, HD), (1, NS, 2048, 2, HPG, HD), (1, NS, 1, AG, 128)]


def kernel(**inputs):
    import concourse.bacc as bacc
    from concourse.bass_utils import run_bass_kernel_spmd

    nc = bacc.Bacc("TRN2", target_bir_lowering=False, num_devices=1)
    arrays, ins, consts = {}, {}, {}
    for name in _INS:
        a = np.ascontiguousarray(inputs[name])
        arrays[f"in_{name}"] = a
        ins[name] = nc.dram_tensor(f"in_{name}", a.shape, mybir.dt.from_np(a.dtype), kind="ExternalInput").ap()
    for name, a in shape_constants().items():
        arrays[f"const_{name}"] = a
        consts[name] = nc.dram_tensor(f"const_{name}", a.shape, F32, kind="ExternalInput").ap()
    outs = [nc.dram_tensor(f"out_{i}", shape, F32, kind="ExternalOutput").ap() for i, shape in enumerate(_OUTS)]
    build(nc, ins, consts, outs)
    r = run_bass_kernel_spmd(nc, [arrays], core_ids=[0])
    return tuple(r.results[0][f"out_{i}"] for i in range(len(_OUTS)))
```

```python
import math
from contextlib import ExitStack

import concourse.bass as bass
import numpy as np
from concourse import mybir

F32 = mybir.dt.float32
F32R = mybir.dt.float32r
BF16 = mybir.dt.bfloat16
I32 = mybir.dt.int32
U32 = mybir.dt.uint32
ALU = mybir.AluOpType
ACT = mybir.ActivationFunctionType
AX = mybir.AxisListType

P = 128
D = 1024
KD = D // P
SEQ = 256
NS = 8
NT = SEQ + NS
TILES = ((0, 128), (128, 128), (256, NS))
PAIRS = ((128, 1), (512, 4), (2048, 16))
NG = len(PAIRS)
HPG = 4
NH = NG * HPG
HD = 64
BW = NH * HD
REL_BUCKETS = 32
REL_MAX_DIST = 2048
AG = 4
NM = 256
CH = 4
CD = 128
E = 32
TOPK = 4
EPS = 1e-6
NEG = -1e30
LIMIT = 7.0
ALPHA = 1.702
C_SCALE = 1.0 / math.sqrt(CD)
B_SCALE = 1.0 / math.sqrt(HD)
SLOTS = 64
PASSES = -(-NT // SLOTS)
CHUNKS = KD + KD // 2
RAW = 8
HALVES = 2 * KD
SPLIT = 4
DOWN = 4
NATIVE = KD - DOWN
SPLITS = HALVES + DOWN
PARTS = 3
HANK = 384
QO, KO, VO, UO, ZO, CO, GO = 0, BW, 2 * BW, 3 * BW, 3 * BW + 512, 3 * BW + 1024, 3 * BW + 1536


def t5_bucket(dist):
    dist = np.maximum(np.asarray(dist), 0)
    exact = REL_BUCKETS // 2
    ratio = np.log(np.maximum(dist, exact) / exact) / math.log(REL_MAX_DIST / exact)
    large = np.minimum(exact + (ratio * (REL_BUCKETS - exact)).astype(np.int32), REL_BUCKETS - 1)
    return np.where(dist < exact, dist, large).astype(np.int32)


def shape_constants():
    c = np.zeros((P, 4 * P + 3 + E + 1), np.float32)
    c[:, 0:P] = np.eye(P)
    c[:, P:2 * P] = np.triu(np.ones((P, P)))
    c[:, 2 * P:3 * P] = np.triu(np.ones((P, P)), 1)
    c[:, 3 * P:4 * P] = np.eye(P)[::-1]
    c[:, 4 * P] = c[:, 4 * P + 1] = 1
    c[:NS, 4 * P + 2] = 1
    c[np.arange(PARTS * E), 4 * P + 3 + np.arange(PARTS * E) % E] = 1
    hank = np.zeros((REL_BUCKETS + 1, NG, HANK), np.float32)
    dist = 2 * P - 1 - np.arange(HANK)
    for g, (window, dilation) in enumerate(PAIRS):
        ok = (dist >= 0) & (dist % dilation == 0) & (dist <= window)
        hank[t5_bucket(dist), g, np.arange(HANK)] = ok
        hank[REL_BUCKETS, g] = np.where(ok, 0, NEG)
    samp = np.zeros((REL_BUCKETS, NG + 1, P), np.float32)
    for g, (window, dilation) in enumerate(PAIRS):
        samp[t5_bucket((P - np.arange(P)) * dilation), g, np.arange(P)] = 1
    samp[t5_bucket(0), NG] = 1
    return {"square": c, "hankel": hank.reshape(REL_BUCKETS + 1, -1), "sample": samp.reshape(REL_BUCKETS, -1)}


def mixer_blocks(w_in, w_mem_kv, w_branch_a, w_branch_b, w_branch_c, w_out):
    def cols(w, a, b):
        return w[0, :, a:b].rearrange("(k p) c -> p k c", p=P)

    def whole(w, p):
        return w[0].rearrange("(k p) c -> p k c", p=p)

    out = [("memk", cols(w_mem_kv, 0, 512)), ("memv", cols(w_mem_kv, 512, 1024))]
    out += [("in0", cols(w_in, 0, 512)), ("in1", cols(w_in, 512, 1024)), ("in2", cols(w_in, 1024, 1536))]
    out += [("v0", cols(w_in, VO, VO + 512)), ("v1", cols(w_in, VO + 512, VO + 768))]
    out += [("qc", cols(w_in, CO, CO + 512)), ("zv", cols(w_in, ZO, ZO + 512)), ("zu", cols(w_in, UO, UO + 512))]
    for n, (i, w, p) in {"a": (0, w_branch_a, P), "c": (2, w_branch_c, P), "b": (1, w_branch_b, HD)}.items():
        g = GO + i * D
        out += [("g" + n + "0", cols(w_in, g, g + 512)), ("w" + n, whole(w, p)), ("g" + n + "1", cols(w_in, g + 512, g + D))]
    out += [("o0", cols(w_out, 0, 512)), ("o1", cols(w_out, 512, 1024))]
    return out


def schedule():
    s = [("vec",), ("wsp",)] + [("rel", g) for g in range(NG)] + [("sbias",)]
    s += [("memT", k) for k in range(KD)] + [("kc", h) for h in range(CH)] + [("xT", k) for k in range(KD)]
    s += [("vc", t) for t in range(2)] + [("kct", t) for t in range(2)]
    s += [("q", m) for m in range(6)] + [("k", m) for m in range(6)]
    s += [("v", t, 0) for t in range(3)] + [("v", t, 1) for t in range(3)]
    s += [("kt", t, n) for t in range(3) for n in range(2)] + [("qc", m) for m in range(4)]
    s += [("qs", 0), ("qs", 1), ("qcs",), ("vts",), ("selfb",)]
    big = [("zv", t) for t in range(3)] + [("zu", m) for m in range(4)]
    for b in range(NS):
        if b == 3:
            s += [("norm_v",)]
        s += [("sk", b, 0), ("sk", b, 1), ("skc", b)]
        if b < len(big):
            s += [big[b]]
    s += [("vat",), ("sp", 0), ("sp", 1), ("sp", 2), ("sp", 3), ("slog",)]
    units = [("C", h, t) for t in range(2) for h in range(CH)] + [("B", h, t) for t in range(2) for h in range(HPG)]
    for n in range(len(units) + 2):
        if n < len(units):
            s += [("score", n, units[n])]
        if n < 16:
            s += [("p" if n % 2 == 0 else "g", "a", n // 2)]
        if 1 <= n <= len(units):
            s += [("turn", n - 1, units[n - 1])]
        if n >= 2:
            s += [("mix", n - 2, units[n - 2])]
        if n == 4:
            s += [("ssum",)]
    for b in range(NS):
        s += [("sv", b)]
    for br in "cb":
        if br == "b":
            s += [("bias",)]
        for m in range(KD):
            s += [("p", br, m), ("g", br, m)]
    s += [("wo", t, n) for n in range(2) for t in range(3)]
    s += [("norm_f",)] + [("hT", k) for k in range(KD)] + [("parts",)]
    s += [("rt", t) for t in range(3)] + [("top",), ("pos",)]
    return s


ROTATING = {"vec", "wsp", "rel", "sbias", "memT", "kc", "xT", "vc", "kct", "q", "k", "v", "kt", "qc", "qs", "qcs", "vts",
            "selfb", "sk", "skc", "zv", "zu", "vat", "sp", "p", "g", "ssum", "sv", "wo", "hT", "rt", "pos"}
LAST_USE = {("kc", 3): 0, ("vc", 1): 1, ("q", 3): 2, ("k", 1): 3, ("k", 5): 4, ("v", 2, 0): 5, ("v", 2, 1): 6, ("qc", 3): 7,
            ("zv", 2): 8, ("zu", 3): 9}
for _n, _br in enumerate("acb"):
    LAST_USE[("g", _br, 3)] = 10 + 3 * _n
    LAST_USE[("p", _br, 7)] = 11 + 3 * _n
    LAST_USE[("g", _br, 7)] = 12 + 3 * _n
LAST_USE[("wo", 2, 0)] = 19
LAST_USE[("wo", 2, 1)] = 20


def here(nc):
    return nc.sbuf_base


def build(nc, I, C, O):
    blocks = mixer_blocks(*(I[n] for n in ("w_in", "w_mem_kv", "w_branch_a", "w_branch_b", "w_branch_c", "w_out")))
    block_at = {name: n for n, (name, _) in enumerate(blocks)}
    steps = schedule()
    job = {s: n for n, s in enumerate([s for s in steps if s[0] in ROTATING])}
    last_job = {n: job[s] + 1 for s, n in LAST_USE.items()}
    caches = [I[f"cache_win{g}_kv"] for g in range(NG)]

    with ExitStack() as ctx:
        def sb(name, shape, dt=F32):
            return ctx.enter_context(nc.sbuf_tensor(name, shape, dt))

        def sem(name):
            return ctx.enter_context(nc.semaphore(name))

        scratch = sb("scratch", [P, 4 * 2048])
        split = nc.alloc_sbuf_tensor_at("split", [P, SPLIT, 2, D], F32R, offset=here(nc) - 4 * 2048 * 4)
        ring = sb("ring", [P, 8 * 2048])

        def block_view(name, p=P):
            n = block_at[name] % 4
            k = blocks[block_at[name]][1].shape[1]
            c = blocks[block_at[name]][1].shape[2]
            return ring[0:p, n * 4096:n * 4096 + k * c].rearrange("p (k c) -> p k c", k=k)

        def chunk_slot(k):
            return 2 + k % 4 if k < KD else (k - 2) % RAW

        def chunk_view(k):
            s = chunk_slot(k)
            return ring[:, s * 2048:(s + 1) * 2048]

        def split_piece(q):
            return {HALVES - 3: (KD - 1, 0), HALVES - 2: (KD - 2, 1)}.get(q, (q // 2, q % 2))

        def split_source(q):
            k, half = split_piece(q)
            return chunk_view(k)[:, half * D:(half + 1) * D]

        def split_done(k):
            return {KD - 2: HALVES - 1}.get(k, 2 * (k + 1))

        kv_b = [scratch[:, n * 1792:n * 1792 + 768].rearrange("p (g c) -> p g c", g=NG) for n in range(2)]
        kv_c = [scratch[:, n * 1792 + 768:(n + 1) * 1792].rearrange("p (t c) -> p t c", t=2) for n in range(2)]
        probs = [scratch[:, 3584 + n * 768:3584 + (n + 1) * 768] for n in range(2)]
        probs_t = [scratch[:, 5120 + n * 768:5120 + (n + 1) * 768] for n in range(2)]
        mem_tok = scratch[:, 3584:3584 + 2048].rearrange("p (t c) -> p t c", t=2)
        prod = scratch[:, 6656:6656 + 1024]

        hT = sb("hT", [P, KD, NT])
        acc = hT
        merged_at = here(nc)
        merged = sb("merged", [P, KD, NT])
        memT = merged[:, :, 0:NM]
        x1 = sb("x1", [P, 3, D])
        hank = x1[:, :, :].rearrange("p t c -> p (t c)").rearrange("p (h k) -> p h k", h=NH)
        qk = sb("qk", [P, 12, NT])
        qT, kT = qk[:, 0:6, :], qk[:, 6:12, :]
        qcT = sb("qcT", [P, CH, NT])
        kvt = sb("kvt", [P, 2 * 3 * BW])
        k_tok = kvt[:, 0:3 * BW].rearrange("p (t c) -> p t c", t=3)
        v_tok = kvt[:, 3 * BW:6 * BW].rearrange("p (t c) -> p t c", t=3)
        kc = sb("kc", [P, CH * NM + 2 * 1024])
        kcT = kc[:, 0:CH * NM].rearrange("p (h m) -> p h m", h=CH)
        kvc = kc[:, CH * NM:].rearrange("p (t c) -> p t c", t=2)
        uT = sb("uT", [P, AG, NT])
        va = sb("va", [P, 3, 512])
        bT_all = sb("bT", [P, HPG * NT])
        bT = bT_all[0:HD, :].rearrange("p (h t) -> p h t", h=HPG)
        lnw = bT_all[:, 0:1024].rearrange("p (a c) -> p a c", a=2)
        sq = sb("sq", [P, 4 * P + 3 + E + 1])
        expert_row = sq[0:PARTS * E, 4 * P + 3:]
        ident, triu, before, flip, valid = (sq[:, 0:P], sq[:, P:2 * P], sq[:, 2 * P:3 * P], sq[:, 3 * P:4 * P],
                                            sq[:, 4 * P:4 * P + 3])
        ones = sb("ones", [P, P])
        wspT = sb("wspT", [P, AG, P])
        wsp = sb("wsp", [P, AG, P])
        bsp = sb("bsp", [P, AG, P])
        w00 = sb("w00", [P, AG])
        vecr = sb("vecr", [3 * KD, P])
        vec = sb("vec", [P, 3 * KD])
        g_mix, g_mem, g_ffn = vec[:, 0:KD], vec[:, KD:2 * KD], vec[:, 2 * KD:3 * KD]
        rel = sb("rel", [REL_BUCKETS + 1, NH])
        selh = va[0:REL_BUCKETS + 1, :, :].rearrange("p t c -> p (t c)")[:, 0:NG * HANK].rearrange("p (g x) -> p g x", g=NG)
        pair = sb("pair", [P, 2 * NT])
        sels = pair[0:REL_BUCKETS, 0:(NG + 1) * P].rearrange("p (g x) -> p g x", g=NG + 1)
        hrow = scratch[0:HPG, 6656:6656 + NG * HANK].rearrange("p (g x) -> p g x", g=NG)
        stat = sb("stat", [P, 40])
        bn = sb("bn", [P, 3, 6])
        bna = sb("bna", [P, 3, 2])
        flat = merged[:, :, :].rearrange("p k t -> p (k t)")
        qs, slf = flat[0:NS, 0:BW + 512], flat[0:NS, BW + 512:2 * BW + 512]
        sbias = sb("sbias", [P, 2 * NH])
        slog = sb("slog", [NS, NH])
        sdiag = sb("sdiag", [NS, NS, NH])
        samp = sb("samp", [P, NS * NH + NS * 2 * CH])
        sB, sC = samp[:, 0:NS * NH], samp[:, NS * NH:]
        smax = sb("smax", [P, NS * NH + NS * 2 * CH])
        stop = sb("stop", [P, NS * HPG + NS * CH])
        stot = sb("stot", [P, NS * HPG + NS * CH])
        sself = sb("sself", [P, NS * NH])
        vts = sb("vts", [HD, NH, NS])
        vself = sb("vself", [HD, HPG, NS])
        th = [sb(f"th{n}", [P, NT]) for n in range(2)]
        tmp = [pair[:, n * NT:(n + 1) * NT] for n in range(2)]
        wr = sb("wr", [P, KD, E])
        br = sb("br", [P, E])

        flat_qk = qk[:, :, :].rearrange("p a b -> p (a b)")
        xr = flat_qk[:, 0:3 * D].rearrange("p (t c) -> p t c", t=3)
        h_tok = flat_qk[:, 0:2 * D]
        xparts = kvt[:].bitcast(BF16).rearrange("p (a t c) -> p a t c", a=PARTS, t=3)
        brow = kc[0:E, 0:3 * D]
        gate, up, th_g, actT = (kc[:, n * 512:(n + 1) * 512].rearrange("p (k s) -> p k s", k=KD) for n in range(4))
        y_tok = kc[:, 2 * D:3 * D]
        bias = va[:, :, :].rearrange("p t c -> p (t c)").bitcast(BF16)
        gfin = qcT[:, :, :].rearrange("p a b -> p (a b)")[:, 0:D]
        gT = bT_all[:, 0:NT]
        sel_g = bT_all[:, 264:648].rearrange("p (t s) -> p t s", t=3)
        sel_p = bT_all[:, 648:744].bitcast(BF16).rearrange("p (t s) -> p t s", t=3)
        sel_b = bT_all[:, 744:808].bitcast(BF16)
        xg = wsp[:, :, :].rearrange("p a b -> p (a b)").rearrange("p (k s) -> p k s", k=KD)
        xsplit = nc.alloc_sbuf_tensor_at("xsplit", [P, KD, 2 * SLOTS], F32R, offset=merged_at)
        asplit = nc.alloc_sbuf_tensor_at("asplit", [P, KD, 2 * SLOTS], F32R, offset=merged_at + 4 * KD * 2 * SLOTS)
        small = uT[:, :, :].rearrange("p a b -> p (a b)")
        lg = small[:, 0:96].rearrange("p (t e) -> p t e", t=3)
        mx8 = small[:, 96:120].rearrange("p (t e) -> p t e", t=3)
        idf = small[:, 120:144].rearrange("p (t e) -> p t e", t=3)
        gk = small[:, 144:156].rearrange("p (t j) -> p t j", t=3)
        gsum = small[:, 156:159]
        eq = small[:, 192:192 + 384].rearrange("p (t e j) -> p t e j", t=3, e=E)
        msk = small[:, 576:672].rearrange("p (t e) -> p t e", t=3)
        gw = small[:, 672:768].rearrange("p (t e) -> p t e", t=3)
        posm = small[:, 768:768 + 99].rearrange("p (t e) -> p t e", t=3)
        most = small[0:1, 870:871]
        iota = sb("iota", [P, SLOTS * PASSES])
        idx = sb("idx", [P, 3, 8], U32)
        over = sb("over", [1, 1], I32)

        psum = ctx.enter_context(nc.psum_tensor("psum", [P, 8 * 512], F32))
        bank = [psum[:, n * 512:(n + 1) * 512] for n in range(4)]
        wide = [psum[:, (4 + 2 * n) * 512:(6 + 2 * n) * 512] for n in range(2)]
        p_h, p_y, p_s = psum[:, 0:4 * 512], wide[0], (wide[1][:, 0:512], wide[1][:, 512:1024])
        p_x = p_s[0]
        p_a = [p[:, 0:NT] for p in (p_s[0], p_s[1], wide[0][:, 0:512], wide[0][:, 512:1024])]
        p_hT = p_h.rearrange("p (a k s) -> p a k s", a=2, k=KD)
        rel_rows = nc.dram_tensor("rel_rows", [NG, HPG, HANK], F32)

        s_sq, s_vecr, s_wsp, s_rel, s_sels, s_lnw, s_bsp, s_w00 = (sem("in_" + n) for n in (
            "square", "vectors", "wsp", "rel", "sample", "lnw", "bsp", "w00"))
        s_router_in, s_gfin_in, s_brow_in = sem("in_router"), sem("in_gfin"), sem("in_brow")
        s_mem_in, s_x_in, s_xagain = sem("in_mem"), sem("in_x"), sem("in_x_again")
        s_block_in = [sem(f"block_in{n}") for n in range(4)]
        s_chunk_in = [sem(f"chunk_in{n}") for n in range(RAW)]
        s_down_used = sem("down_used")
        s_job = sem("job_done")
        s_taken = [sem(f"taken{n}") for n in range(3)]
        s_done = {n: sem("ready_" + n) for n in (
            "ones", "vec", "wspT", "rel_aug", "hrow", "sbias", "xn", "memn", "memT", "xT", "kcT", "kvc", "q", "k", "v", "ktok", "qc",
            "qs", "vts", "sdiag", "selfb", "sk", "va", "vraw", "uT", "aT", "sexp", "sprob", "parmax", "bs", "cs", "th", "merged",
            "x1", "xr", "hTf", "logits", "masks", "posm", "bexp", "lgs")}
        s_hstore, s_hank, s_kv_in, s_kv_used, s_out = sem("hankel_stored"), sem("in_hankel"), sem("kv_in"), sem("kv_used"), sem("out")
        s_kvin = [sem(f"kv_in{n}") for n in range(2)]
        s_kvout, s_kvcout, s_vaout = sem("out_kv"), sem("out_memkv"), sem("out_chunk_v")
        s_copy = sem("out_shift")
        s_score, s_max, s_exp, s_prob, s_turned, s_pt, s_mixed, s_mixout = (sem("att_" + n) for n in (
            "scores", "max", "exp", "probs", "turned", "probs_t", "mixed", "out"))
        s_ss, s_ms, s_rt, s_rs = sem("sum_squares"), sem("mean_square"), sem("root"), sem("inv_root")
        s_tmax, s_texp = sem("top_shifted"), sem("top_exp")
        s_accout = sem("experts_summed")
        s_dve, s_act = sem("dve_step"), sem("act_step")
        s_p, s_pg, s_selb, s_gath, s_xf, s_xhi, s_xg, s_hi, s_lo, s_split_used, s_h, s_hturn, s_low, s_gate, s_th, s_actv, s_ahi, s_asplit, s_ytok, \
            s_gturn, s_gT, s_scat, s_acc, s_loop, s_y, s_upg = (sem("moe_" + n) for n in (
                "select", "gated_select", "bias_select", "gathered", "x_rows", "x_high", "x_split", "high", "low", "split_used",
                "h", "h_turned", "low_turned", "gate", "tanh", "act", "act_high", "act_split", "y_tok", "g_turned", "gT", "scattered", "added", "dve_step", "y", "up_times_gate"))
        s_bhi, s_bmid, s_bias, s_bres, s_parts, s_pstep = (sem("bias_" + n) for n in ("high", "mid", "done", "rest", "x_parts", "x_step"))
        s_iota = sem("iota")
        s_carry = sem("waits_carried")
        s_finj, s_fin, s_finT = sem("final_turned"), sem("final_rows"), sem("final_added")

        def taken(eng, *s):
            eng.wait_ge(s_taken[job[s] % 3], job[s] // 3 + 1)

        block = ctx.enter_context(nc.Block())

        @block.sync
        def _(sp):
            with nc.allow_non_contiguous_dma(reason="small vectors"):
                sp.dma_start(mem_tok, I["mem_prompt"][0].rearrange("(t p) c -> p t c", p=P)).then_inc(s_mem_in, 16)
                sp.dma_start(x1[:, 0:2, :], I["x_prompt"][0].rearrange("(t p) c -> p t c", p=P)).then_inc(s_x_in, 16)
                sp.dma_start(x1[0:NS, 2, :], I["x_sample"][:, 0, :]).then_inc(s_x_in, 16)
            copies = []
            for b in range(NS):
                copies.append((2, slice(b, b + 1)))
                if b == 3:
                    copies.append((1, slice(0, 4)))
            copies += [(1, slice(4, 8)), (0, slice(0, 8))]

            def shift(g, bs):
                w = PAIRS[g][0]
                src = caches[g][0, bs, 1:w].rearrange("b w a h c -> b (w a h c)")
                dst = O[6 + g][0, bs, 0:w - 1].rearrange("b w a h c -> b (w a h c)")
                sp.dma_start(dst, src).then_inc(s_copy, 16)

            for n, (name, src) in enumerate(blocks):
                if n >= 4:
                    sp.wait_ge(s_job, last_job[n - 4])
                sp.dma_start(block_view(name, src.shape[0]), src).then_inc(s_block_in[n % 4], 16)
                if n == 0:
                    sp.wait_ge(s_vecr, 48)
                    sp.wait_ge(s_wsp, 16)
                    sp.wait_ge(s_rel, 32)
                    sp.wait_ge(s_sels, 16)
                if 10 <= n and copies:
                    shift(*copies.pop(0))
                if name == "gc1":
                    sp.wait_ge(s_mixed, 2 * (CH + HPG))
                    sp.dma_start(x1[:, 0:2, :], I["x_prompt"][0].rearrange("(t p) c -> p t c", p=P)).then_inc(s_xagain, 16)
                    sp.dma_start(x1[0:NS, 2, :], I["x_sample"][:, 0, :]).then_inc(s_xagain, 16)
                    sp.wait_ge(s_kvcout, 16)
                    sp.dma_start(brow[:, 0:2 * D], I["b_gate_up"][0]).then_inc(s_brow_in, 16)
                    sp.dma_start(brow[:, 2 * D:3 * D], I["b_down"][0]).then_inc(s_brow_in, 16)
            for c in copies:
                shift(*c)

            def chunk(e, k):
                s = chunk_slot(k)
                if k < KD:
                    src = I["w_gate_up"][0, e, k * P:(k + 1) * P, :]
                    dst = chunk_view(k)
                else:
                    r = (k - KD) * 2 * P
                    src = I["w_down"][0, e, r:r + 2 * P, :].rearrange("(j p) c -> p j c", p=P)
                    dst = chunk_view(k).rearrange("p (j c) -> p j c", j=2)
                sp.dma_start(dst, src).then_inc(s_chunk_in[s], 16)

            def chunk_dyn(e, k):
                s = chunk_slot(k)
                if k < KD:
                    src = I["w_gate_up"][0, bass.ds(e, 1), k * P:(k + 1) * P, :].rearrange("e p c -> p (e c)")
                    dst = chunk_view(k)
                else:
                    r = (k - KD) * 2 * P
                    src = I["w_down"][0, bass.ds(e, 1), r:r + 2 * P, :].rearrange("e (j p) c -> p (e j) c", p=P)
                    dst = chunk_view(k).rearrange("p (j c) -> p j c", j=2)
                sp.dma_start(dst, src).then_inc(s_chunk_in[s], 16)

            for k in range(CHUNKS):
                if k < KD and k >= 4:
                    sp.wait_ge(s_lo, split_done(k - 4))
                else:
                    sp.wait_ge(s_job, last_job[{2: 17, 4: 18, 6: 19, 0: 20}[chunk_slot(k) // 2 * 2]])
                chunk(0, k)

            def one_expert(n33, n32, e):
                for k in range(CHUNKS):
                    if k == CHUNKS - 1:
                        sp.wait_ge(s_y, n33 + 1)
                    elif k >= KD + DOWN // 2:
                        sp.wait_ge(s_down_used, n32 * (NATIVE - 1) + (2 * (k - KD + 1) - DOWN - NATIVE + 1))
                    elif k >= KD:
                        sp.wait_ge(s_lo, n32 * SPLITS + (split_done(k) - SPLITS))
                    elif k >= 4:
                        sp.wait_ge(s_lo, n32 * SPLITS + split_done(k - 4))
                    else:
                        sp.wait_ge(s_lo, n32 * SPLITS + (split_done(k + 4) - SPLITS))
                    chunk_dyn(e, k)

            with sp.Fori(1, E) as e:
                one_expert(e, e, e)
            sp.wait_ge(s_done["posm"], 1)
            flag = sp.value_load(over[0:1, 0:1], min_val=0, max_val=NT)
            with sp.If(flag > SLOTS):
                with sp.Fori(1, PASSES) as ps:
                    with sp.Fori(0, E) as e:
                        one_expert(ps * (E + 1) + e, ps * E + e, e)
            sp.wait_ge(s_fin, 1)
            sp.dma_start(O[0][0, 0:P], x1[:, 0, :]).then_inc(s_out, 16)
            sp.wait_ge(s_fin, 2)
            sp.dma_start(O[0][0, P:2 * P], x1[:, 1, :]).then_inc(s_out, 16)
            sp.wait_ge(s_fin, 3)
            sp.dma_start(O[1][:, 0, :], x1[0:NS, 2, :]).then_inc(s_out, 16)
            sp.wait_ge(s_out, 48)
            sp.wait_ge(s_copy, 16 * 11)

        @block.gpsimd
        def _(pool):
            nc.gpsimd.iota(iota[:], [[1, SLOTS * PASSES]], base=0, channel_multiplier=0,
                           allow_small_or_imprecise_dtypes=True).then_inc(s_iota, 1)
            taken(pool, "rel", NG - 1)
            pool.dma_start(rel_rows[:].rearrange("g h x -> h g x"), hrow).then_inc(s_hstore, 16)
            pool.wait_ge(s_hstore, 16)
            src = bass.AP(rel_rows, 0, [[1, P], [HANK, NH], [1, 2 * P]])
            taken(pool, "xT", KD - 1)
            pool.dma_start(hank, src).then_inc(s_hank, 16)

            def stream(n):
                b, a = n % NS, n // NS
                if n >= 2:
                    pool.wait_ge(s_kv_used, n - 1)
                for g, (w, dil) in enumerate(PAIRS):
                    src = caches[g][0, b, :, a].rearrange("(j r) h c -> j r (h c)", r=dil)[:, 0, :]
                    pool.dma_start(kv_b[n % 2][:, g, :], src).then_inc(s_kvin[n % 2], 16)
                src = I["cache_mem_kv"][0, b, :, a].rearrange("(t p) h c -> p t (h c)", p=P)
                pool.dma_start(kv_c[n % 2], src).then_inc(s_kvin[n % 2], 16)

            stream(0)
            stream(1)
            taken(pool, "kct", 1)
            dst = O[5][0, 0].rearrange("(t p) a h c -> p t (a h c)", p=P)
            pool.dma_start(dst, kvc).then_inc(s_kvcout, 16)
            taken(pool, "v", 2, 1)
            taken(pool, "kt", 2, 1)
            for a, rows in ((0, k_tok), (1, v_tok)):
                for g, (w, _) in enumerate(PAIRS):
                    c = slice(g * 256, (g + 1) * 256)
                    first = 0 if w >= SEQ else 1
                    dst = O[2 + g][0, 0, :, a].rearrange("(t p) h c -> p t (h c)", p=P)
                    pool.dma_start(dst, rows[:, first:2, c]).then_inc(s_kvout, 16)
                    pool.dma_start(O[6 + g][0, :, w - 1, a].rearrange("b h c -> b (h c)"), rows[0:NS, 2, c]).then_inc(s_kvout, 16)
            for n in range(2, NS + 2):
                stream(n)
            pool.wait_ge(s_done["va"], 1)
            pool.dma_start(O[9][0, :, 0].rearrange("b g c -> b (g c)"), va[0:NS, 2, :]).then_inc(s_vaout, 16)
            pool.wait_ge(s_done["lgs"], 1)
            nc.gpsimd.partition_all_reduce(smax[:], samp[:], P, bass.bass_isa.ReduceOp.max).then_inc(s_done["parmax"], 1)
            for n in range(NS + 2, 2 * NS):
                stream(n)
            pool.wait_ge(s_kvcout, 16)
            pool.wait_ge(s_kvout, 16 * 12)
            pool.wait_ge(s_vaout, 16)

        @block.tensor
        def _(pe):
            def mm(out, lhsT, rhs, start=True, stop=True, **kw):
                return nc.tensor.matmul(out, lhsT, rhs, start=start, stop=stop, **kw)

            def turn(out, in_, n):
                return nc.tensor.transpose(out, in_, ident[0:n, 0:n])

            landed = set()

            def weights(name):
                n = block_at[name]
                if name not in landed:
                    pe.wait_ge(s_block_in[n % 4], 16 * (n // 4 + 1))
                    landed.add(name)
                return block_view(name, blocks[n][1].shape[0])

            def wide_tile(out, w, m, rhs, kn=KD):
                for k in range(kn):
                    last = mm(out, w[:, k, m * P:(m + 1) * P], rhs[:, k, :], k == 0, k == kn - 1)
                return last

            def row_tile(out, lhs, w, t, n):
                t0, tn = TILES[t]
                for k in range(KD):
                    last = mm(out[0:tn, 0:n], lhs[:, k, t0:t0 + tn], w[:, k, 0:n], k == 0, k == KD - 1)
                return last

            pe.wait_ge(s_sq, 16)
            pe.wait_ge(s_done["ones"], 2)
            for s in steps:
                kind, a = s[0], s[1:]
                if kind in ROTATING:
                    n = job[s]
                    o = bank[n % 3]
                    if n >= 3:
                        pe.wait_ge(s_taken[n % 3], n // 3)
                if kind == "vec":
                    pe.wait_ge(s_vecr, 48)
                    last = turn(o[:, 0:3 * KD], vecr[:], 3 * KD)
                elif kind == "wsp":
                    pe.wait_ge(s_wsp, 16)
                    for g in range(AG):
                        last = turn(o[:, g * P:(g + 1) * P], wsp[:, g, :], P)
                elif kind == "rel":
                    g, = a
                    pe.wait_ge(s_rel, 32)
                    last = mm(o[0:HPG, 0:HANK], rel[:, g * HPG:(g + 1) * HPG], selh[:, g, :])
                elif kind == "sbias":
                    pe.wait_ge(s_sels, 16)
                    for g in range(NG):
                        h4 = slice(g * HPG, (g + 1) * HPG)
                        mm(o[:, h4], sels[:, g, :], rel[0:REL_BUCKETS, h4])
                    last = mm(o[:, NH:2 * NH], sels[:, NG, :], rel[0:REL_BUCKETS, :])
                elif kind == "memT":
                    k, = a
                    pe.wait_ge(s_done["memn"], 1)
                    for t in range(2):
                        last = turn(o[:, t * P:(t + 1) * P], mem_tok[:, t, k * P:(k + 1) * P], P)
                elif kind == "xT":
                    k, = a
                    pe.wait_ge(s_done["xn"], 1)
                    for t, (t0, tn) in enumerate(TILES):
                        last = turn(o[:, t0:t0 + tn], x1[0:tn, t, k * P:(k + 1) * P], tn)
                elif kind == "kc":
                    taken(pe, "memT", KD - 1)
                    last = wide_tile(o[:, 0:NM], weights("memk"), a[0], memT)
                elif kind == "vc":
                    t, = a
                    w = weights("memv")
                    for k in range(KD):
                        last = mm(o, memT[:, k, t * P:(t + 1) * P], w[:, k, :], k == 0, k == KD - 1)
                elif kind == "kct":
                    t, = a
                    taken(pe, "kc", CH - 1)
                    for h in range(CH):
                        last = turn(o[:, h * P:(h + 1) * P], kcT[:, h, t * P:(t + 1) * P], P)
                elif kind in ("q", "k"):
                    taken(pe, "xT", KD - 1)
                    c = a[0] + (0 if kind == "q" else 6)
                    last = wide_tile(o[:, 0:NT], weights(f"in{c // 4}"), c % 4, hT)
                elif kind == "v":
                    t, n = a
                    last = row_tile(o, hT, weights(f"v{n}"), t, (512, 256)[n])
                elif kind == "kt":
                    t, n = a
                    t0, tn = TILES[t]
                    taken(pe, "k", 5)
                    for i in range(3):
                        last = turn(o[0:tn, i * P:(i + 1) * P], kT[:, 3 * n + i, t0:t0 + tn], P)
                elif kind == "qc":
                    last = wide_tile(o[:, 0:NT], weights("qc"), a[0], hT)
                elif kind == "qs":
                    n, = a
                    taken(pe, "q", 5)
                    for i in range(3):
                        last = turn(o[0:NS, i * P:(i + 1) * P], qT[:, 3 * n + i, SEQ:NT], P)
                elif kind == "qcs":
                    taken(pe, "qc", CH - 1)
                    for h in range(CH):
                        last = turn(o[0:NS, h * P:(h + 1) * P], qcT[:, h, SEQ:NT], P)
                elif kind == "vts":
                    taken(pe, "v", 2, 1)
                    for h in range(NH):
                        last = turn(o[0:HD, h * NS:(h + 1) * NS], v_tok[0:NS, 2, h * HD:(h + 1) * HD], NS)
                elif kind == "selfb":
                    pe.wait_ge(s_done["sdiag"], 1)
                    last = mm(o[:, 0:NS * NH], ones[0:NS, :], sdiag[:].rearrange("p b h -> p (b h)"))
                elif kind == "sk":
                    b, n = a
                    taken(pe, "qcs")
                    last = mm(o[:, 0:384], ident[0:NS, b:b + 1].to_broadcast([NS, P]), qs[:, n * 384:(n + 1) * 384])
                elif kind == "skc":
                    last = mm(o, ident[0:NS, a[0]:a[0] + 1].to_broadcast([NS, P]), qs[:, BW:BW + 512])
                elif kind == "zv":
                    last = row_tile(o, hT, weights("zv"), a[0], 512)
                elif kind == "zu":
                    last = wide_tile(o[:, 0:NT], weights("zu"), a[0], hT)
                elif kind == "vat":
                    pe.wait_ge(s_done["va"], 1)
                    for g in range(AG):
                        last = turn(o[:, g * NS:(g + 1) * NS], va[0:NS, 2, g * P:(g + 1) * P], NS)
                elif kind == "sp":
                    g, = a
                    for t in range(2):
                        last = mm(o[:, t * P:(t + 1) * P], va[:, t, g * P:(g + 1) * P], wspT[:, g, :])
                elif kind == "p":
                    br_, m = a
                    if br_ == "a":
                        pe.wait_ge(s_done["aT"], 1 + AG)
                        last = wide_tile(o[:, 0:NT], weights("wa"), m, uT, AG)
                    elif br_ == "c":
                        taken(pe, "sv", NS - 1)
                        pe.wait_ge(s_mixout, 2 * (CH + HPG))
                        last = wide_tile(o[:, 0:NT], weights("wc"), m, qcT, CH)
                    else:
                        taken(pe, "sv", NS - 1)
                        last = wide_tile(o[:, 0:NT], weights("wb"), m, bT, HPG)
                elif kind == "g":
                    br_, m = a
                    last = wide_tile(o[:, 0:NT], weights(f"g{br_}{m // 4}"), m % 4, hT)
                elif kind == "score":
                    n, (what, h, t) = a
                    if n >= 1:
                        pe.wait_ge(s_exp, n)
                    if what == "C":
                        mm(wide[0][:, 0:NM], qcT[:, h, t * P:(t + 1) * P], kcT[:, h, :]).then_inc(s_score, 1)
                    else:
                        pe.wait_ge(s_hank, 16)
                        nk = (t + 1) * P
                        for g in range(NG):
                            hh = g * HPG + h
                            r = slice(HD * (hh % 2), HD * (hh % 2) + HD)
                            so = wide[0][:, g * 256:g * 256 + nk]
                            mm(so, flip, hank[:, hh, 2 * P - nk:2 * P], True, False)
                            last = mm(so, qT[r, hh // 2, t * P:(t + 1) * P], kT[r, hh // 2, 0:nk], False, True)
                        last.then_inc(s_score, 1)
                elif kind == "turn":
                    n, (what, h, t) = a
                    pe.wait_ge(s_prob, n + 1)
                    if n >= 1:
                        pe.wait_ge(s_pt, n)
                    i = 0
                    for g in range(1 if what == "C" else NG):
                        for j in range(2 if what == "C" else t + 1):
                            last = turn(wide[1][:, i * P:(i + 1) * P], probs[n % 2][:, g * 256 + j * P:g * 256 + (j + 1) * P], P)
                            i += 1
                    last.then_inc(s_turned, 1)
                elif kind == "mix":
                    n, (what, h, t) = a
                    pe.wait_ge(s_pt, n + 1)
                    if n >= 1:
                        pe.wait_ge(s_mixout, n)
                    if what == "C":
                        for j in range(2):
                            last = mm(bank[3][:, 0:P], kvc[:, j, 512 + h * P:512 + (h + 1) * P], probs_t[n % 2][:, j * P:(j + 1) * P],
                                      j == 0, j == 1)
                    else:
                        nb = NG * (t + 1)
                        for i in range(nb):
                            g, j = i // (t + 1), i % (t + 1)
                            hh = g * HPG + h
                            last = mm(bank[3][0:HD, 0:P], v_tok[:, j, hh * HD:(hh + 1) * HD], probs_t[n % 2][:, i * P:(i + 1) * P],
                                      i == 0, i == nb - 1)
                    last.then_inc(s_mixed, 1)
                elif kind == "ssum":
                    pe.wait_ge(s_done["sexp"], 2)
                    last = mm(o[:, 0:NS * (NH + 2 * CH)], ones[:], samp[:])
                elif kind == "sv":
                    b, = a
                    pe.wait_ge(s_done["sprob"], 1)
                    pe.wait_ge(s_kvin[b % 2], 64 * (NS // 2 + b // 2 + 1))
                    pb = sB.rearrange("p (b h) -> p b h", b=NS)
                    pc = sC.rearrange("p (b t h) -> p b t h", b=NS, t=2)
                    for h in range(HPG):
                        for g in range(NG):
                            hh = g * HPG + h
                            mm(o[0:HD, h:h + 1], kv_b[b % 2][:, g, h * HD:(h + 1) * HD], pb[:, b, hh:hh + 1], g == 0, g == NG - 1)
                    for h in range(CH):
                        for j in range(2):
                            last = mm(o[:, HPG + h:HPG + h + 1], kv_c[b % 2][:, j, h * P:(h + 1) * P], pc[:, b, j, h:h + 1],
                                      j == 0, j == 1)
                elif kind == "wo":
                    t, n = a
                    pe.wait_ge(s_done["merged"], 3 * KD)
                    last = row_tile(o, merged, weights(f"o{n}"), t, 512)
                elif kind == "hT":
                    k, = a
                    pe.wait_ge(s_done["xr"], 1)
                    for t, (t0, tn) in enumerate(TILES):
                        last = turn(o[:, t0:t0 + tn], xr[0:tn, t, k * P:(k + 1) * P], tn)
                elif kind == "rt":
                    taken(pe, "hT", KD - 1)
                    pe.wait_ge(s_router_in, 32)
                    last = row_tile(o, merged, wr, a[0], E)
                elif kind == "pos":
                    pe.wait_ge(s_done["masks"], 1)
                    for t in range(3):
                        for u in range(t + 1):
                            mm(o[:, t * E:(t + 1) * E], before if u == t else ones[:], msk[:, u, :], u == 0, u == t)
                    for t in range(3):
                        last = mm(o[0:1, 3 * E:4 * E], ones[:, 0:1], msk[:, t, :], t == 0, t == 2)
                if kind in ROTATING:
                    last.then_inc(s_job, 1)

            for n in range(len(job) - 3, len(job)):
                pe.wait_ge(s_taken[n % 3], n // 3 + 1)

            pe.sem_inc(s_split_used, SPLIT)

            pe.wait_ge(s_pstep, PARTS)

            def gather(count):
                pe.wait_ge(s_p, count)
                for k in range(KD):
                    ks, out = slice(k * P, (k + 1) * P), p_x[:, k * SLOTS:(k + 1) * SLOTS]
                    for t in range(2):
                        for n in range(PARTS):
                            mm(out, xparts[:, n, t, ks], sel_p[:, t, :], t + n == 0, False)
                    last = mm(out, xparts[0:PARTS * E, 0, 2, ks], sel_p[0:PARTS * E, 2, :], False, True)
                last.then_inc(s_gath, 1)

            def scatter(n33, c):
                if c >= 4:
                    pe.wait_ge(s_acc, n33 * KD + (c - 3))
                mm(p_a[c % 4], y_tok[:, c * P:(c + 1) * P], gT).then_inc(s_scat, 1)

            def one_pass(b):
                if not isinstance(b, int):
                    pe.wait_ge(s_acc, b * ((E + 1) * KD))
                gather(b * (E + 1) + 1)
                with pe.Fori(0, E) as i:
                    n33 = b * (E + 1) + i
                    n32 = b * E + i
                    for q in range(HALVES):
                        k, half = split_piece(q)
                        ho = p_h[:, half * D:(half + 1) * D]
                        if q == 0:
                            pe.wait_ge(s_xg, n33 + 1)
                        if q == 3:
                            pe.wait_ge(s_ytok, n33 + 1)
                            pe.wait_ge(s_gT, n33 + 1)
                        if 3 <= q < 3 + KD:
                            scatter(n33, q - 3)
                        if q == KD + 4:
                            pe.wait_ge(s_acc, n33 * KD + 6)
                            pe.wait_ge(s_pg, n32 + 1)
                            pe.sem_inc(s_carry, 1)
                            for t, (t0, tn) in enumerate(TILES):
                                last = turn(p_s[1][:, t0:t0 + tn], sel_g[0:tn, t, :], tn)
                            last.then_inc(s_gturn, 1)
                        pe.wait_ge(s_lo, n32 * SPLITS + (q + 1))
                        for part in range(2):
                            for n in range(2):
                                cs = slice(n * 512, (n + 1) * 512)
                                last = mm(ho[:, cs], xsplit[:, k, :], split[:, q % SPLIT, part, cs], k == 0 and part == 0,
                                          k == KD - 1 and part == 1, skip_group_check=True)
                        last.then_inc(s_split_used, 1)
                        if q == HALVES // 2:
                            pe.wait_ge(s_selb, n32 + 1)
                            for n in range(4):
                                mm(p_h[:, n * 512:(n + 1) * 512], sel_b[0:PARTS * E, :], bias[0:PARTS * E, n * 512:(n + 1) * 512], False, False,
                                   skip_group_check=True)
                    gather(n33 + 2)
                    for half in range(2):
                        pe.wait_ge(s_h, n32 * 2 + (half + 1))
                        pe.sem_inc(s_carry, 1)
                        for k in range(KD):
                            f = half * D + k * P
                            last = turn(p_hT[:, half, k, :], h_tok[:, f:f + P], P)
                        last.then_inc(s_hturn, 1)
                    pe.wait_ge(s_acc, n33 * KD + KD)
                    for n in range(2):
                        mm(p_y[:, n * 512:(n + 1) * 512], sel_b[0:PARTS * E, :], bias[0:PARTS * E, 2 * D + n * 512:2 * D + (n + 1) * 512],
                           True, False, skip_group_check=True)
                    order = [DOWN] + list(range(DOWN)) + list(range(DOWN + 1, KD))
                    for k in order:
                        c = KD + k // 2
                        if k == order[0]:
                            pe.wait_ge(s_actv, n32 + 1)
                        if k >= DOWN:
                            if k % 2 == 0:
                                pe.wait_ge(s_chunk_in[chunk_slot(c)], n32 * 16 + 16)
                            w = chunk_view(c).rearrange("p (j c) -> p j c", j=2)[:, k % 2, :]
                            for n in range(2):
                                cs = slice(n * 512, (n + 1) * 512)
                                last = mm(p_y[0:SLOTS, cs], actT[:, k, :], w[:, cs], False, k == KD - 1, skip_group_check=True)
                            last.then_inc(s_down_used if k < KD - 1 else s_y, 1)
                        else:
                            q = HALVES + k
                            if k == 0:
                                pe.wait_ge(s_asplit, n32 + 1)
                            pe.wait_ge(s_lo, n32 * SPLITS + (q + 1))
                            for part in range(2):
                                for n in range(2):
                                    cs = slice(n * 512, (n + 1) * 512)
                                    last = mm(p_y[:, cs], asplit[:, k, :], split[:, q % SPLIT, part, cs], False, False, skip_group_check=True)
                            last.then_inc(s_split_used, 1)
                last33 = b * (E + 1) + E
                pe.wait_ge(s_ytok, last33 + 1)
                pe.wait_ge(s_gT, last33 + 1)
                for c in range(KD):
                    scatter(last33, c)

            one_pass(0)
            flag = pe.value_load(over[0:1, 0:1], min_val=0, max_val=NT)
            with pe.If(flag > SLOTS):
                with pe.Fori(1, PASSES) as ps:
                    one_pass(ps)
            pe.wait_ge(s_accout, 1)
            for t, (t0, tn) in enumerate(TILES):
                w = wide[t % 2]
                if t == 2:
                    pe.wait_ge(s_finT, 1)
                for k in range(KD):
                    last = turn(w[0:tn, k * P:(k + 1) * P], acc[:, k, t0:t0 + tn], P)
                last.then_inc(s_finj, 1)

        @block.vector
        def _(dve):
            done = [0]

            def seq(ins):
                done[0] += 1
                ins.then_inc(s_dve, 1)
                dve.wait_ge(s_dve, done[0])

            def rms_scale(r, n, count):
                dve.wait_ge(s_ss, count)
                nc.vector.tensor_scalar(r, r, 1.0 / n, EPS, ALU.mult, ALU.add).then_inc(s_ms, 1)

            V = nc.vector
            V.memset(ones[:], 1.0).then_inc(s_done["ones"], 1)
            seq(V.memset(stat[:], 1.0))
            V.memset(rel[REL_BUCKETS:REL_BUCKETS + 1, :], 1.0).then_inc(s_done["ones"], 1)
            rms_scale(stat[:, 0:2], D, 2)
            dve.wait_ge(s_rt, 1)
            seq(V.reciprocal(stat[:, 0:2], stat[:, 0:2]))
            for t in range(2):
                ins = V.tensor_scalar(mem_tok[:, t, :], mem_tok[:, t, :], stat[:, t:t + 1], None, ALU.mult)
                if t == 0:
                    seq(ins)
            ins.then_inc(s_done["memn"], 1)
            rms_scale(stat[:, 2:5], D, 5)
            dve.wait_ge(s_rt, 2)
            seq(V.reciprocal(stat[:, 2:5], stat[:, 2:5]))
            for t, (_, tn) in enumerate(TILES):
                ins = V.tensor_scalar(x1[0:tn, t, :], x1[0:tn, t, :], stat[0:tn, 2 + t:3 + t], None, ALU.mult)
                if t < 2:
                    seq(ins)
            ins.then_inc(s_done["xn"], 1)

            for s in steps:
                kind, a = s[0], s[1:]
                if kind in ROTATING:
                    n = job[s]
                    o = bank[n % 3]
                    free = s_taken[n % 3]

                    def ready(n=n):
                        dve.wait_ge(s_job, n + 1)

                    def own(n=n):
                        dve.wait_ge(s_taken[n % 3], n // 3 + 1)
                if kind == "vec":
                    ready()
                    V.tensor_copy(vec[:], o[:, 0:3 * KD]).then_inc(free, 1)
                    own()
                elif kind == "wsp":
                    ready()
                    V.tensor_tensor(wspT[:], o.rearrange("p (g i) -> p g i", g=AG),
                                        triu.unsqueeze(1).to_broadcast([P, AG, P]), ALU.mult).then_inc(free, 1)
                elif kind == "sbias":
                    ready()
                    V.tensor_copy(sbias[:], o[:, 0:2 * NH]).then_inc(free, 1)
                    own()
                elif kind == "memT":
                    k, = a
                    ready()
                    V.tensor_scalar(memT[:, k, :], o[:, 0:NM], g_mem[:, k:k + 1], None, ALU.mult).then_inc(free, 1)
                elif kind == "xT":
                    k, = a
                    ready()
                    V.tensor_scalar(hT[:, k, :], o[:, 0:NT], g_mix[:, k:k + 1], None, ALU.mult).then_inc(free, 1)
                elif kind == "q":
                    ready()
                    V.tensor_scalar(qT[:, a[0], :], o[:, 0:NT], B_SCALE, None, ALU.mult).then_inc(free, 1)
                elif kind == "kt":
                    t, n2 = a
                    tn = TILES[t][1]
                    ready()
                    V.tensor_copy(k_tok[0:tn, t, n2 * 384:(n2 + 1) * 384], o[0:tn, 0:384]).then_inc(free, 1)
                elif kind == "qc":
                    ready()
                    V.tensor_copy(qcT[:, a[0], :], o[:, 0:NT]).then_inc(free, 1)
                elif kind in ("qs", "qcs"):
                    c, w = (a[0] * 384, 384) if kind == "qs" else (BW, 512)
                    ready()
                    V.tensor_copy(qs[:, c:c + w], o[0:NS, 0:w]).then_inc(free, 1)
                    own()
                    if kind == "qcs":
                        seq(V.tensor_tensor(slf, qs[:, 0:BW], k_tok[0:NS, 2, :], ALU.mult))
                        seq(V.tensor_reduce(slog[:], slf.rearrange("p (h c) -> p h c", c=HD), AX.X, ALU.add))
                        seq(V.tensor_tensor(slog[:], slog[:], sbias[0:NS, NH:2 * NH], ALU.add))
                        V.tensor_tensor(sdiag[:], ident[0:NS, 0:NS].unsqueeze(2).to_broadcast([NS, NS, NH]),
                                        slog[:].unsqueeze(1).to_broadcast([NS, NS, NH]), ALU.mult).then_inc(s_done["sdiag"], 1)
                elif kind == "vts":
                    ready()
                    V.tensor_copy(vts[:], o[0:HD, 0:NH * NS].rearrange("p (h b) -> p h b", h=NH)).then_inc(free, 1)
                    own()
                elif kind == "selfb":
                    ready()
                    V.tensor_copy(sself[:], o[:, 0:NS * NH]).then_inc(free, 1)
                    own()
                elif kind == "sk":
                    b, n2 = a
                    if n2 == 0:
                        dve.wait_ge(s_kvin[b % 2], 64 * (b // 2 + 1))
                    ready()
                    kk = kv_b[b % 2].rearrange("p g c -> p (g c)")[:, n2 * 384:(n2 + 1) * 384]
                    V.tensor_tensor(prod[:, 0:384], kk, o[:, 0:384], ALU.mult).then_inc(free, 1)
                    own()
                    seq(V.tensor_reduce(sB[:, b * NH + 6 * n2:b * NH + 6 * n2 + 6], prod[:, 0:384].rearrange("p (h c) -> p h c", c=HD),
                                        AX.X, ALU.add))
                elif kind == "skc":
                    b, = a
                    ready()
                    V.tensor_tensor(prod.rearrange("p (t c) -> p t c", t=2), kv_c[b % 2], o.unsqueeze(1).to_broadcast([P, 2, 512]),
                                        ALU.mult).then_inc(free, 1)
                    own()
                    dve.sem_inc(s_kv_used, 1)
                    seq(V.tensor_reduce(sC[:, b * 8:(b + 1) * 8], prod.rearrange("p (h c) -> p h c", c=CD), AX.X, ALU.add))
                elif kind == "norm_v":
                    taken(dve, "zv", 2)
                    for t, (_, tn) in enumerate(TILES):
                        seq(V.bn_stats(bn[0:tn, t, :], va[0:tn, t, :]))
                        seq(V.bn_aggr(bna[0:tn, t, :], bn[0:tn, t, :]))
                        seq(V.tensor_scalar(stat[0:tn, 8 + t:9 + t], bna[0:tn, t, 1:2], EPS, None, ALU.add))
                    dve.sem_inc(s_ms, 1)
                    dve.wait_ge(s_rt, 3)
                    seq(V.reciprocal(stat[:, 8:11], stat[:, 8:11]))
                    dve.wait_ge(s_lnw, 32)
                    for t, (_, tn) in enumerate(TILES):
                        v = va[0:tn, t, :]
                        seq(V.tensor_scalar(v, v, bna[0:tn, t, 0:1], stat[0:tn, 8 + t:9 + t], ALU.subtract, ALU.mult))
                        seq(V.tensor_tensor(v, v, lnw[0:tn, 0, :], ALU.mult))
                        seq(V.tensor_tensor(v, v, lnw[0:tn, 1, :], ALU.add))
                    dve.sem_inc(s_done["va"], 1)
                elif kind == "vat":
                    dve.wait_ge(s_bsp, 16)
                    dve.wait_ge(s_w00, 16)
                    taken(dve, "zu", AG - 1)
                    ready()
                    t3 = tmp[0][:, 0:AG * NS].rearrange("p (g b) -> p g b", g=AG)
                    V.tensor_tensor(t3, o[:, 0:AG * NS].rearrange("p (g b) -> p g b", g=AG),
                                        w00[:].unsqueeze(2).to_broadcast([P, AG, NS]), ALU.mult).then_inc(free, 1)
                    own()
                    seq(V.tensor_tensor(t3, t3, bsp[:, :, 0:1].to_broadcast([P, AG, NS]), ALU.add))
                    V.tensor_tensor(uT[:, :, SEQ:NT], uT[:, :, SEQ:NT], t3, ALU.mult).then_inc(s_done["aT"], 1)
                elif kind == "sp":
                    g, = a
                    ready()
                    t2 = tmp[1][:, 0:SEQ].rearrange("p (t i) -> p t i", t=2)
                    V.tensor_tensor(t2, o[:, 0:SEQ].rearrange("p (t i) -> p t i", t=2),
                                        bsp[:, g, :].unsqueeze(1).to_broadcast([P, 2, P]), ALU.add).then_inc(free, 1)
                    own()
                    seq(V.tensor_tensor(uT[:, g, 0:SEQ], uT[:, g, 0:SEQ], tmp[1][:, 0:SEQ], ALU.mult))
                    dve.sem_inc(s_done["aT"], 1)
                elif kind == "slog":
                    b3 = sB.rearrange("p (b h) -> p b h", b=NS)
                    seq(V.tensor_scalar(sC, sC, C_SCALE, None, ALU.mult))
                    seq(V.tensor_tensor(b3, b3, sbias[:, 0:NH].unsqueeze(1).to_broadcast([P, NS, NH]), ALU.add))
                    dve.sem_inc(s_done["lgs"], 1)
                    dve.wait_ge(s_done["parmax"], 1)
                    mB = smax[:, 0:NS * NH]
                    seq(V.tensor_tensor(mB, mB, sself[:], ALU.max))
                    m4 = mB.rearrange("p (b g h) -> p b h g", b=NS, g=NG)
                    m5 = smax[:, NS * NH:].rearrange("p (b t h) -> p b h t", b=NS, t=2)
                    top3 = stop[:, 0:NS * HPG].rearrange("p (b h) -> p b h", b=NS)
                    top4 = stop[:, NS * HPG:].rearrange("p (b h) -> p b h", b=NS)
                    seq(V.tensor_reduce(top3, m4, AX.X, ALU.max))
                    seq(V.tensor_reduce(top4, m5, AX.X, ALU.max))
                    s4 = sB.rearrange("p (b g h) -> p b g h", b=NS, g=NG)
                    f4 = sself[:].rearrange("p (b g h) -> p b g h", b=NS, g=NG)
                    c4 = sC.rearrange("p (b t h) -> p b t h", b=NS, t=2)
                    seq(V.tensor_tensor(s4, s4, top3.unsqueeze(2).to_broadcast([P, NS, NG, HPG]), ALU.subtract))
                    seq(V.tensor_tensor(f4, f4, top3.unsqueeze(2).to_broadcast([P, NS, NG, HPG]), ALU.subtract))
                    seq(V.tensor_tensor(c4, c4, top4.unsqueeze(2).to_broadcast([P, NS, 2, CH]), ALU.subtract))
                    dve.sem_inc(s_done["lgs"], 1)
                elif kind == "ssum":
                    ready()
                    seq(V.tensor_tensor(smax[:, 0:NS * NH], o[:, 0:NS * NH], sself[:], ALU.add))
                    V.tensor_copy(smax[:, NS * NH:], o[:, NS * NH:NS * (NH + 2 * CH)]).then_inc(free, 1)
                    own()
                    t3 = stot[:, 0:NS * HPG].rearrange("p (b h) -> p b h", b=NS)
                    t4 = stot[:, NS * HPG:].rearrange("p (b h) -> p b h", b=NS)
                    seq(V.tensor_reduce(t3, smax[:, 0:NS * NH].rearrange("p (b g h) -> p b h g", b=NS, g=NG), AX.X, ALU.add))
                    seq(V.tensor_reduce(t4, smax[:, NS * NH:].rearrange("p (b t h) -> p b h t", b=NS, t=2), AX.X, ALU.add))
                    seq(V.reciprocal(stot[:], stot[:]))
                    s4 = sB.rearrange("p (b g h) -> p b g h", b=NS, g=NG)
                    f4 = sself[:].rearrange("p (b g h) -> p b g h", b=NS, g=NG)
                    c4 = sC.rearrange("p (b t h) -> p b t h", b=NS, t=2)
                    seq(V.tensor_tensor(s4, s4, t3.unsqueeze(2).to_broadcast([P, NS, NG, HPG]), ALU.mult))
                    seq(V.tensor_tensor(f4, f4, t3.unsqueeze(2).to_broadcast([P, NS, NG, HPG]), ALU.mult))
                    seq(V.tensor_tensor(c4, c4, t4.unsqueeze(2).to_broadcast([P, NS, 2, CH]), ALU.mult))
                    dve.sem_inc(s_done["sprob"], 1)
                    pf = sself[0:HD, :].rearrange("p (b h) -> p h b", b=NS)
                    seq(V.tensor_tensor(vts[:], vts[:], pf, ALU.mult))
                    seq(V.tensor_reduce(vself[:], vts[:].rearrange("p (g h) b -> p h b g", g=NG), AX.X, ALU.add))
                elif kind == "sv":
                    b, = a
                    ready()
                    seq(V.tensor_tensor(bT[:, :, SEQ + b:SEQ + b + 1], o[0:HD, 0:HPG].unsqueeze(2), vself[:, :, b:b + 1], ALU.add))
                    V.tensor_copy(qcT[:, :, SEQ + b:SEQ + b + 1], o[:, HPG:HPG + CH].unsqueeze(2)).then_inc(free, 1)
                    dve.sem_inc(s_kv_used, 1)
                elif kind == "score":
                    n2, (what, h, t) = a
                    dve.wait_ge(s_score, n2 + 1)
                    m = stat[:, 16 + n2 % 2:17 + n2 % 2]
                    if what == "C":
                        seq(V.tensor_reduce(m, wide[0][:, 0:NM], AX.X, ALU.max))
                        V.tensor_scalar(m, m, -C_SCALE, None, ALU.mult).then_inc(s_max, 1)
                    else:
                        nk = (t + 1) * P
                        src = wide[0][:, 0:768].rearrange("p (g k) -> p g k", g=NG)[:, :, 0:nk]
                        seq(V.tensor_reduce(m, src, AX.XY, ALU.max))
                        V.tensor_scalar(m, m, -1.0, None, ALU.mult).then_inc(s_max, 1)
                    dve.wait_ge(s_exp, n2 + 1)
                    r = stat[:, 18 + n2 % 2:19 + n2 % 2]
                    seq(V.reciprocal(r, r))
                    if what == "C":
                        pv = probs[n2 % 2][:, 0:NM]
                    else:
                        pv = probs[n2 % 2].rearrange("p (g k) -> p g k", g=NG)[:, :, 0:(t + 1) * P]
                    V.tensor_scalar(pv, pv, r, None, ALU.mult).then_inc(s_prob, 1)
                elif kind == "mix":
                    n2, (what, h, t) = a
                    dve.wait_ge(s_mixed, n2 + 1)
                    ts = slice(t * P, (t + 1) * P)
                    if what == "C":
                        V.tensor_copy(qcT[:, h, ts], bank[3][:, 0:P]).then_inc(s_mixout, 1)
                    else:
                        V.tensor_copy(bT[:, h, ts], bank[3][0:HD, 0:P]).then_inc(s_mixout, 1)
                elif kind == "g":
                    br_, m = a
                    i = "acb".index(br_) * KD + m
                    n = job[("p", br_, m)]
                    o = bank[n % 3]
                    taken(dve, *s)
                    V.scalar_tensor_tensor(tmp[i % 2], th[i % 2][:], 1.0, o[:, 0:NT], ALU.add, ALU.mult).then_inc(s_taken[n % 3], 1)
                    dve.wait_ge(s_taken[n % 3], n // 3 + 1)
                    if br_ == "a":
                        if m == 0:
                            taken(dve, "kct", 1)
                        V.tensor_scalar(merged[:, m, :], tmp[i % 2], 0.5, None, ALU.mult).then_inc(s_done["merged"], 1)
                    else:
                        seq(V.scalar_tensor_tensor(merged[:, m, :], tmp[i % 2], 0.5, merged[:, m, :], ALU.mult, ALU.add))
                        dve.sem_inc(s_done["merged"], 1)
                elif kind == "wo":
                    t, n2 = a
                    tn = TILES[t][1]
                    dve.wait_ge(s_xagain, 32)
                    ready()
                    xs = x1[0:tn, t, n2 * 512:(n2 + 1) * 512]
                    V.tensor_tensor(xs, xs, o[0:tn, :], ALU.add).then_inc(free, 1)
                elif kind == "norm_f":
                    rms_scale(stat[:, 24:27], D, 8)
                    dve.wait_ge(s_rt, 4)
                    seq(V.reciprocal(stat[:, 24:27], stat[:, 24:27]))
                    dve.wait_ge(s_kvout, 16 * 12)
                    seq(V.memset(xparts[0:PARTS * E, 0, 2, :], 0.0))
                    for t, (_, tn) in enumerate(TILES):
                        seq(V.tensor_scalar(xr[0:tn, t, :], x1[0:tn, t, :], stat[0:tn, 24 + t:25 + t], None, ALU.mult))
                    dve.sem_inc(s_done["xr"], 1)
                    seq(V.memset(acc[:], 0.0))
                    seq(V.memset(small[:, 0:880], 0.0))
                    seq(V.memset(sel_b, 0.0))
                elif kind == "bias":
                    dve.wait_ge(s_bhi, 1)
                    V.tensor_tensor(brow, brow, bias[0:E, :], ALU.subtract).then_inc(s_bres, 1)
                    dve.wait_ge(s_bmid, 2)
                    V.tensor_tensor(bias[2 * E:3 * E, :], brow, flat_qk.bitcast(BF16)[0:E, 0:3 * D], ALU.subtract).then_inc(s_bias, 1)
                elif kind == "hT":
                    k, = a
                    ready()
                    V.tensor_scalar(merged[:, k, :], o[:, 0:NT], g_ffn[:, k:k + 1], None, ALU.mult).then_inc(free, 1)
                elif kind == "rt":
                    t, = a
                    tn = TILES[t][1]
                    ready()
                    dve.wait_ge(s_router_in, 32)
                    V.tensor_tensor(lg[0:tn, t, :], o[0:tn, 0:E], br[0:tn, :], ALU.add).then_inc(free, 1)
                    own()
                elif kind == "parts":
                    for i in range(2):
                        dve.wait_ge(s_pstep, i + 1)
                        for t, (_, tn) in enumerate(TILES):
                            seq(V.tensor_tensor(xr[0:tn, t, :], xr[0:tn, t, :], xparts[0:tn, i, t, :], ALU.subtract))
                        dve.sem_inc(s_parts, 1)
                elif kind == "top":
                    for t in range(3):
                        seq(V.max(mx8[:, t, :], lg[:, t, :]))
                        seq(V.max_index(idx[:, t, :], mx8[:, t, :], lg[:, t, :]))
                    seq(V.tensor_copy(idf, idx[:]))
                    V.tensor_tensor(gk, mx8[:, :, 0:TOPK], mx8[:, :, 0:1].to_broadcast([P, 3, TOPK]), ALU.subtract).then_inc(s_tmax, 1)
                    dve.wait_ge(s_texp, 1)
                    seq(V.tensor_reduce(gsum, gk, AX.X, ALU.add))
                    seq(V.reciprocal(gsum, gsum))
                    seq(V.tensor_tensor(gk, gk, gsum.unsqueeze(2).to_broadcast([P, 3, TOPK]), ALU.mult))
                    dve.wait_ge(s_iota, 1)
                    seq(V.tensor_tensor(eq, iota[:, 0:E].unsqueeze(1).unsqueeze(3).to_broadcast([P, 3, E, TOPK]),
                                        idf[:, :, 0:TOPK].unsqueeze(2).to_broadcast([P, 3, E, TOPK]), ALU.is_equal))
                    seq(V.tensor_reduce(msk, eq, AX.X, ALU.add))
                    seq(V.tensor_tensor(msk, msk, valid.unsqueeze(2).to_broadcast([P, 3, E]), ALU.mult))
                    dve.sem_inc(s_done["masks"], 1)
                    seq(V.tensor_tensor(eq, eq, gk.unsqueeze(2).to_broadcast([P, 3, E, TOPK]), ALU.mult))
                    seq(V.tensor_reduce(gw, eq, AX.X, ALU.add))
                elif kind == "pos":
                    ready()
                    seq(V.memset(posm, -1.0))
                    seq(V.scalar_tensor_tensor(posm[:, :, 0:E], o[:, 0:3 * E].rearrange("p (t e) -> p t e", t=3), 1.0, msk, ALU.add, ALU.mult))
                    seq(V.tensor_scalar(posm[:, :, 0:E], posm[:, :, 0:E], -1.0, None, ALU.add))
                    for n in range(1, PARTS):
                        seq(V.tensor_copy(posm[n * E:n * E + NS, 2, :], posm[0:NS, 2, :]))
                    seq(V.tensor_reduce(most, o[0:1, 3 * E:4 * E], AX.X, ALU.max))
                    V.tensor_copy(over[:], most).then_inc(free, 1)
                    own()
                    dve.sem_inc(s_done["posm"], 1)

            STEPS = 3

            def select_p(b, e):
                first = iota[:, b * SLOTS:(b + 1) * SLOTS] if isinstance(b, int) else iota[:, bass.ds(b * SLOTS, SLOTS)]
                place = posm[:, :, e:e + 1] if isinstance(e, int) else posm[:, :, bass.ds(e, 1)]
                V.tensor_tensor(sel_p, first.unsqueeze(1).to_broadcast([P, 3, SLOTS]), place.to_broadcast([P, 3, SLOTS]),
                                ALU.is_equal).then_inc(s_p, 1)

            def take_x(n33):
                dve.wait_ge(s_gath, n33 + 1)
                V.tensor_tensor(xg, p_x.rearrange("p (k s) -> p k s", k=KD), g_ffn.unsqueeze(2).to_broadcast([P, KD, SLOTS]),
                                ALU.mult).then_inc(s_xf, 1)

            def split_x(n33):
                dve.wait_ge(s_xhi, n33 + 1)
                V.tensor_tensor(xsplit[:, :, SLOTS:2 * SLOTS], xg, xsplit[:, :, 0:SLOTS].bitcast(F32), ALU.subtract).then_inc(s_xg, 1)

            def add_up(n33, c):
                dve.wait_ge(s_scat, n33 * KD + (c + 1))
                V.tensor_tensor(acc[:, c, :], p_a[c % 4], acc[:, c, :], ALU.add).then_inc(s_acc, 1)

            def one_pass(b):
                select_p(b, 0)
                V.memset(gT, 0.0).then_inc(s_gT, 1)
                take_x(b * (E + 1))
                dve.wait_ge(s_xf, b * (E + 1) + 1)
                V.memset(p_y, 0.0).then_inc(s_y, 1)
                split_x(b * (E + 1))
                with dve.Fori(0, E) as i:
                    n33 = b * (E + 1) + i
                    n32 = b * E + i
                    step = [0]

                    def link(ins):
                        step[0] += 1
                        ins.then_inc(s_loop, 1)
                        dve.wait_ge(s_loop, n32 * STEPS + step[0])

                    def low(q, w):
                        dve.wait_ge(s_hi, n32 * SPLITS + (q + 1))
                        V.tensor_tensor(split[:, q % SPLIT, 1, :], w, split[:, q % SPLIT, 0, :].bitcast(F32), ALU.subtract).then_inc(s_lo, 1)

                    for q in range(SPLITS - 1):
                        low(q, split_source(q))
                        if q == 3:
                            dve.wait_ge(s_p, n33 + 1)
                            V.tensor_tensor(sel_g.rearrange("p t (a s) -> p t a s", a=2), sel_p.unsqueeze(2).to_broadcast([P, 3, 2, SLOTS]),
                                            gw[:, :, bass.ds(i, 1)].unsqueeze(3).to_broadcast([P, 3, 2, SLOTS]), ALU.mult).then_inc(s_pg, 1)
                            dve.wait_ge(s_y, n33 + 1)
                            V.tensor_copy(sel_b[0:PARTS * E, 0:SLOTS],
                                          expert_row[:, bass.ds(i, 1)].to_broadcast([PARTS * E, SLOTS])).then_inc(s_selb, 1)
                            dve.wait_ge(s_pg, n32 + 1)
                            select_p(b, i + 1)
                        if 6 <= q < 6 + KD:
                            add_up(n33, q - 6)
                    hi, lo = slice(0, SLOTS), slice(SLOTS, 2 * SLOTS)
                    dve.wait_ge(s_low, n32 * 2 + 1)
                    link(V.tensor_tensor(gate, p_hT[:, 0, :, hi], gate, ALU.add))
                    V.tensor_scalar(gate, gate, LIMIT, 0.5, ALU.min, ALU.mult).then_inc(s_gate, 1)
                    dve.wait_ge(s_low, n32 * 2 + 2)
                    link(V.tensor_tensor(up, p_hT[:, 1, :, hi], up, ALU.add))
                    link(V.tensor_scalar(up, up, LIMIT, -LIMIT, ALU.min, ALU.max))
                    dve.wait_ge(s_gate, n32 + 1)
                    V.scalar_tensor_tensor(up, up, 1.0, gate, ALU.add, ALU.mult).then_inc(s_upg, 1)
                    dve.wait_ge(s_upg, n32 + 1)
                    dve.wait_ge(s_th, n32 + 1)
                    V.scalar_tensor_tensor(actT, th_g, 1.0, up, ALU.add, ALU.mult).then_inc(s_actv, 1)
                    dve.wait_ge(s_ahi, n32 + 1)
                    V.tensor_tensor(asplit[:, :, lo], actT, asplit[:, :, hi].bitcast(F32), ALU.subtract).then_inc(s_asplit, 1)
                    low(SPLITS - 1, split_source(SPLITS - 1))
                    take_x(n33 + 1)
                    split_x(n33 + 1)
                    assert step[0] == STEPS
                for c in range(KD):
                    add_up(b * (E + 1) + E, c)
                dve.wait_ge(s_acc, b * ((E + 1) * KD) + (E + 1) * KD)

            one_pass(0)
            flag = dve.value_load(over[0:1, 0:1], min_val=0, max_val=NT)
            with dve.If(flag > SLOTS):
                with dve.Fori(1, PASSES) as ps:
                    one_pass(ps)
            dve.sem_inc(s_accout, 1)
            for t, (_, tn) in enumerate(TILES):
                dve.wait_ge(s_finj, t + 1)
                V.tensor_tensor(x1[0:tn, t, :], x1[0:tn, t, :], wide[t % 2][0:tn, :], ALU.add).then_inc(s_finT, 1)
            rms_scale(stat[:, 28:31], D, 11)
            dve.wait_ge(s_rt, 5)
            seq(V.reciprocal(stat[:, 28:31], stat[:, 28:31]))
            dve.wait_ge(s_gfin_in, 16)
            for t, (_, tn) in enumerate(TILES):
                V.scalar_tensor_tensor(x1[0:tn, t, :], x1[0:tn, t, :], stat[0:tn, 28 + t:29 + t], gfin[0:tn, :], ALU.mult,
                                       ALU.mult).then_inc(s_fin, 1)

        @block.scalar
        def _(act):
            A = nc.scalar
            done = [0]

            def seq(ins):
                done[0] += 1
                ins.then_inc(s_act, 1)
                act.wait_ge(s_act, done[0])

            with nc.allow_non_contiguous_dma(reason="small vectors"):
                act.dma_start(sq[:], C["square"]).then_inc(s_sq, 16)
                for n, name in enumerate(("norm_mix", "norm_mem", "norm_ffn")):
                    act.dma_start(vecr[n * KD:(n + 1) * KD, :], I[name][0].rearrange("(k p) -> k p", p=P)).then_inc(s_vecr, 16)
                act.dma_start(wsp[:], I["w_spatial"][0].rearrange("g i j -> i g j")).then_inc(s_wsp, 16)
                act.dma_start(rel[0:REL_BUCKETS, :], I["rel_bias"]).then_inc(s_rel, 16)
                act.dma_start(selh.rearrange("p g x -> p (g x)"), C["hankel"]).then_inc(s_rel, 16)
                act.dma_start(sels.rearrange("p g x -> p (g x)"), C["sample"]).then_inc(s_sels, 16)
                act.dma_start(lnw[:, 0, :], I["ln_v_g"].to_broadcast([P, 512])).then_inc(s_lnw, 16)
                act.dma_start(lnw[:, 1, :], I["ln_v_b"].to_broadcast([P, 512])).then_inc(s_lnw, 16)
                act.dma_start(bsp[:].rearrange("p g i -> p (g i)"),
                              I["b_spatial"].rearrange("d g i -> d (g i)").to_broadcast([P, AG * P])).then_inc(s_bsp, 16)
                act.dma_start(w00[:], I["w_spatial"][:, :, 0, 0].to_broadcast([P, AG])).then_inc(s_w00, 16)
                act.dma_start(wr[:], I["w_router"][0].rearrange("(k p) e -> p k e", p=P)).then_inc(s_router_in, 16)
                act.dma_start(br[:], I["b_router"].to_broadcast([P, E])).then_inc(s_router_in, 16)

            def squares(dst, src, junk):
                A.activation(junk, src, ACT.Square, accum_out=dst).then_inc(s_ss, 1)

            junk = merged[:, :, :].rearrange("p a b -> p (a b)")
            act.wait_ge(s_dve, 1)
            act.wait_ge(s_mem_in, 16)
            for t in range(2):
                squares(stat[:, t:t + 1], mem_tok[:, t, :], junk[:, t * D:(t + 1) * D])
            act.wait_ge(s_ms, 1)
            A.activation(stat[:, 0:2], stat[:, 0:2], ACT.Sqrt).then_inc(s_rt, 1)
            act.wait_ge(s_x_in, 32)
            junk2 = qk[:, :, :].rearrange("p a b -> p (a b)")
            for t, (_, tn) in enumerate(TILES):
                squares(stat[0:tn, 2 + t:3 + t], x1[0:tn, t, :], junk2[0:tn, t * D:(t + 1) * D])
            act.wait_ge(s_ms, 2)
            A.activation(stat[:, 2:5], stat[:, 2:5], ACT.Sqrt).then_inc(s_rt, 1)

            for s in steps:
                kind, a = s[0], s[1:]
                if kind in ROTATING:
                    n = job[s]
                    o = bank[n % 3]
                    free = s_taken[n % 3]

                    def take(out, in_, name, n=n, free=free):
                        act.wait_ge(s_job, n + 1)
                        A.copy(out, in_).then_inc(free, 1)
                if kind == "rel":
                    take(hrow[:, a[0], :], o[0:HPG, 0:HANK], "hrow")
                elif kind == "kc":
                    take(kcT[:, a[0], :], o[:, 0:NM], "kcT")
                elif kind == "vc":
                    take(kvc[:, a[0], 512:1024], o, "kvc")
                elif kind == "kct":
                    take(kvc[:, a[0], 0:512], o, "kvc")
                elif kind == "k":
                    take(kT[:, a[0], :], o[:, 0:NT], "k")
                elif kind == "v":
                    t, n2 = a
                    tn, w = TILES[t][1], (512, 256)[n2]
                    take(v_tok[0:tn, t, n2 * 512:n2 * 512 + w], o[0:tn, 0:w], "v")
                elif kind == "zv":
                    t, = a
                    tn = TILES[t][1]
                    act.wait_ge(s_job, n + 1)
                    A.activation(va[0:tn, t, :], o[0:tn, :], ACT.Gelu_apprx_tanh).then_inc(free, 1)
                elif kind == "zu":
                    act.wait_ge(s_job, n + 1)
                    A.activation(uT[:, a[0], :], o[:, 0:NT], ACT.Gelu_apprx_tanh).then_inc(free, 1)
                elif kind == "norm_v":
                    act.wait_ge(s_ms, 3)
                    A.activation(stat[:, 8:11], stat[:, 8:11], ACT.Sqrt).then_inc(s_rt, 1)
                elif kind == "slog":
                    act.wait_ge(s_done["lgs"], 2)
                    A.activation(samp[:], samp[:], ACT.Exp).then_inc(s_done["sexp"], 1)
                    A.activation(sself[:], sself[:], ACT.Exp).then_inc(s_done["sexp"], 1)
                elif kind == "score":
                    n2, (what, h, t) = a
                    act.wait_ge(s_max, n2 + 1)
                    m, r = stat[:, 16 + n2 % 2:17 + n2 % 2], stat[:, 18 + n2 % 2:19 + n2 % 2]
                    if n2 >= 2:
                        act.wait_ge(s_turned, n2 - 1)
                    if what == "C":
                        A.activation(probs[n2 % 2][:, 0:NM], wide[0][:, 0:NM], ACT.Exp, bias=m, scale=C_SCALE,
                                     accum_out=r).then_inc(s_exp, 1)
                    else:
                        nk = (t + 1) * P
                        A.activation(probs[n2 % 2].rearrange("p (g k) -> p g k", g=NG)[:, :, 0:nk],
                                     wide[0][:, 0:768].rearrange("p (g k) -> p g k", g=NG)[:, :, 0:nk], ACT.Exp, bias=m,
                                     accum_out=r).then_inc(s_exp, 1)
                elif kind == "turn":
                    n2, (what, h, t) = a
                    w = 2 * P if what == "C" else NG * (t + 1) * P
                    act.wait_ge(s_turned, n2 + 1)
                    if n2 >= 2:
                        act.wait_ge(s_mixed, n2 - 1)
                    A.copy(probs_t[n2 % 2][:, 0:w], wide[1][:, 0:w]).then_inc(s_pt, 1)
                elif kind == "g":
                    br_, m = a
                    i = "acb".index(br_) * KD + m
                    act.wait_ge(s_job, n + 1)
                    if i >= 2:
                        act.wait_ge(s_done["merged"], i - 1)
                    A.activation(th[i % 2][:], o[:, 0:NT], ACT.Tanh, scale=0.5).then_inc(free, 1)
                elif kind == "norm_f":
                    taken(act, "wo", 2, 1)
                    for t, (_, tn) in enumerate(TILES):
                        squares(stat[0:tn, 24 + t:25 + t], x1[0:tn, t, :], junk[0:tn, 0:D] if t == 0 else flat_qk[0:tn, (t - 1) * D:t * D])
                    act.wait_ge(s_ms, 4)
                    A.activation(stat[:, 24:27], stat[:, 24:27], ACT.Sqrt).then_inc(s_rt, 1)
                    act.dma_start(gfin, I["norm_final"].rearrange("(a d) -> a d", a=1).to_broadcast([P, D])).then_inc(s_gfin_in, 16)
                elif kind == "bias":
                    act.wait_ge(s_brow_in, 32)
                    act.wait_ge(s_vaout, 16)
                    mid = flat_qk.bitcast(BF16)[0:E, 0:3 * D]
                    A.copy(bias[0:E, :], brow).then_inc(s_bhi, 1)
                    act.wait_ge(s_bres, 1)
                    A.copy(mid, brow).then_inc(s_bmid, 1)
                    A.copy(bias[E:2 * E, :], brow).then_inc(s_bmid, 1)
                elif kind == "parts":
                    for i in range(PARTS):
                        if i == 0:
                            act.wait_ge(s_done["xr"], 1)
                        else:
                            act.wait_ge(s_parts, i)
                        if i == 1:
                            taken(act, "hT", KD - 1)
                        for t, (_, tn) in enumerate(TILES):
                            ins = A.copy(xparts[0:tn, i, t, :], xr[0:tn, t, :])
                        if i > 0:
                            ins = A.copy(xparts[i * E:i * E + NS, 0, 2, :], xr[0:NS, 2, :])
                        ins.then_inc(s_pstep, 1)
                elif kind == "top":
                    act.wait_ge(s_tmax, 1)
                    A.activation(gk, gk, ACT.Exp).then_inc(s_texp, 1)

            def high_x(n33):
                act.wait_ge(s_xf, n33 + 1)
                A.copy(xsplit[:, :, 0:SLOTS], xg).then_inc(s_xhi, 1)

            def take_y(n33):
                act.wait_ge(s_y, n33 + 1)
                A.copy(y_tok, p_y).then_inc(s_ytok, 1)

            def one_pass(b):
                high_x(b * (E + 1))
                with act.Fori(0, E) as i:
                    n33 = b * (E + 1) + i
                    n32 = b * E + i
                    def high(q):
                        k, half = split_piece(q)
                        if half == 0:
                            act.wait_ge(s_chunk_in[chunk_slot(k)], n32 * 32 + 16 * (k // 4 + 1) if k < KD else n32 * 16 + 16)
                        act.wait_ge(s_split_used, n32 * SPLITS + (q + 1))
                        A.copy(split[:, q % SPLIT, 0, :], split_source(q)).then_inc(s_hi, 1)

                    for q in range(SPLITS - 1):
                        high(q)
                        if q == SPLIT - 1:
                            take_y(n33)
                    for half in range(2):
                        act.wait_ge(s_split_used, n32 * SPLITS + (SPLIT + HALVES + 2 * (half - 1)))
                        A.copy(h_tok[:, half * D:(half + 1) * D], p_h[:, half * D:(half + 1) * D]).then_inc(s_h, 1)
                    act.wait_ge(s_hturn, n32 * 2 + 1)
                    A.copy(gate, p_hT[:, 0, :, SLOTS:2 * SLOTS]).then_inc(s_low, 1)
                    act.wait_ge(s_hturn, n32 * 2 + 2)
                    A.copy(up, p_hT[:, 1, :, SLOTS:2 * SLOTS]).then_inc(s_low, 1)
                    act.wait_ge(s_gate, n32 + 1)
                    A.activation(th_g, gate, ACT.Tanh, scale=ALPHA).then_inc(s_th, 1)
                    act.wait_ge(s_gturn, n32 + 1)
                    A.copy(gT, p_s[1][:, 0:NT]).then_inc(s_gT, 1)
                    act.wait_ge(s_actv, n32 + 1)
                    A.copy(asplit[:, :, 0:SLOTS], actT).then_inc(s_ahi, 1)
                    high(SPLITS - 1)
                    high_x(n33 + 1)
                take_y(b * (E + 1) + E)

            one_pass(0)
            flag = act.value_load(over[0:1, 0:1], min_val=0, max_val=NT)
            with act.If(flag > SLOTS):
                with act.Fori(1, PASSES) as ps:
                    one_pass(ps)
            for t, (_, tn) in enumerate(TILES):
                act.wait_ge(s_finT, t + 1)
                squares(stat[0:tn, 28 + t:29 + t], x1[0:tn, t, :], xr[0:tn, t, :])
            act.wait_ge(s_ms, 5)
            A.activation(stat[:, 28:31], stat[:, 28:31], ACT.Sqrt).then_inc(s_rt, 1)


_INS = ["x_prompt", "x_sample", "cache_win0_kv", "cache_win1_kv", "cache_win2_kv", "cache_mem_kv", "mem_prompt", "rel_bias", "norm_mix",
        "norm_mem", "w_in", "ln_v_g", "ln_v_b", "w_spatial", "b_spatial", "w_mem_kv", "w_branch_a", "w_branch_b", "w_branch_c", "w_out",
        "norm_ffn", "w_router", "b_router", "w_gate_up", "b_gate_up", "w_down", "b_down", "norm_final"]
_OUTS = [(1, SEQ, D), (NS, 1, D), (1, 1, 128, 2, HPG, HD), (1, 1, 256, 2, HPG, HD), (1, 1, 256, 2, HPG, HD), (1, 1, NM, 2, CH, CD),
         (1, NS, 128, 2, HPG, HD), (1, NS, 512, 2, HPG, HD), (1, NS, 2048, 2, HPG, HD), (1, NS, 1, AG, 128)]


def kernel(**inputs):
    import concourse.bacc as bacc
    from concourse.bass_utils import run_bass_kernel_spmd

    nc = bacc.Bacc("TRN2", target_bir_lowering=False, num_devices=1)
    arrays, ins, consts = {}, {}, {}
    for name in _INS:
        a = np.ascontiguousarray(inputs[name])
        arrays[f"in_{name}"] = a
        ins[name] = nc.dram_tensor(f"in_{name}", a.shape, mybir.dt.from_np(a.dtype), kind="ExternalInput").ap()
    for name, a in shape_constants().items():
        arrays[f"const_{name}"] = a
        consts[name] = nc.dram_tensor(f"const_{name}", a.shape, F32, kind="ExternalInput").ap()
    outs = [nc.dram_tensor(f"out_{i}", shape, F32, kind="ExternalOutput").ap() for i, shape in enumerate(_OUTS)]
    build(nc, ins, consts, outs)
    r = run_bass_kernel_spmd(nc, [arrays], core_ids=[0])
    return tuple(r.results[0][f"out_{i}"] for i in range(len(_OUTS)))
```
